# Optimizing a Trainium2 kernel written in Bass

```python
import jax, jax.numpy as jnp
from jax import lax
import numpy as np

D_MODEL = 1024
BATCH = 1
SEQ = 256
DEPTH = 1
DEC_BATCH = 1
DEC_SEQ = 1024
PAST_LEN = 128

H_RET = 4
DK_RET = 128
DV_RET = 128
RET_CHUNK = 128
H_HG = 4
DK_HG = 128
DV_HG = 128
HG_CHUNK = 64
N_EXPERTS = 16
CAPACITY_FACTOR = 2
D_EXPERT = 2048
ROPE_BASE = 10000.0
NORM_EPS = 1e-6
RET_QK = H_RET * DK_RET
RET_V = H_RET * DV_RET
HG_K = H_HG * DK_HG
HG_V = H_HG * DV_HG
COL_SIZES = [RET_QK, RET_QK, RET_V, RET_V, HG_K, HG_V, HG_K, HG_K, HG_V, D_MODEL, D_MODEL]
D_IN = int(sum(COL_SIZES))

kernel_name = "hybrid_bidir_retention_hgrn2_ec_moe"

def rms_norm(x, g):
    xf = x.astype(jnp.float32)
    y = xf * lax.rsqrt(jnp.mean(xf * xf, axis=-1, keepdims=True) + NORM_EPS)
    return (y * g.astype(jnp.float32)).astype(x.dtype)

def split_cols(u):
    offs = np.cumsum(COL_SIZES)[:-1].tolist()
    return jnp.split(u, offs, axis=-1)

def heads(t, n_heads):
    return t.reshape(t.shape[0], t.shape[1], n_heads, -1)

def flip_seq(t):
    return jnp.flip(t, axis=1)

def to_chunks(t, c):
    b, s, h, d = t.shape
    return t.reshape(b, s // c, c, h, d).transpose(0, 3, 1, 2, 4)

def from_chunks(t):
    b, h, n, c, d = t.shape
    return t.transpose(0, 2, 3, 1, 4).reshape(b, n * c, h, d)

def rotary(x):
    s, hd = x.shape[1], x.shape[-1]
    half = hd // 2
    inv = 1.0 / (ROPE_BASE ** (jnp.arange(half, dtype=jnp.float32) / half))
    ang = jnp.arange(s, dtype=jnp.float32)[:, None] * inv[None, :]
    cos = jnp.cos(ang)[None, :, None, :]
    sin = jnp.sin(ang)[None, :, None, :]
    x1, x2 = x[..., :half], x[..., half:]
    return jnp.concatenate([x1 * cos - x2 * sin, x1 * sin + x2 * cos], axis=-1)

def head_layer_norm(y, g):
    mu = jnp.mean(y, axis=-1, keepdims=True)
    yc = y - mu
    yn = yc * lax.rsqrt(jnp.mean(yc * yc, axis=-1, keepdims=True) + NORM_EPS)
    return yn.reshape(y.shape[0], y.shape[1], -1) * g.astype(jnp.float32)

def head_rms_norm(y, g):
    yn = y * lax.rsqrt(jnp.mean(y * y, axis=-1, keepdims=True) + NORM_EPS)
    return yn.reshape(y.shape[0], y.shape[1], -1) * g.astype(jnp.float32)

def retention_dir(q, k, v, log_gamma, strict):
    c = q.shape[3]
    pos = jnp.arange(c, dtype=jnp.float32)
    diff = pos[:, None] - pos[None, :]
    mask = (diff > 0) if strict else (diff >= 0)
    decay = jnp.where(mask[None], jnp.exp(log_gamma[:, None, None] * jnp.maximum(diff, 0.0)[None]), 0.0)
    scores = jnp.einsum('bhnid,bhnjd->bhnij', q, k) * decay[None, :, None]
    intra = jnp.einsum('bhnij,bhnjv->bhniv', scores, v)
    lg = log_gamma[:, None]
    k_dec = k * jnp.exp(lg * (c - 1 - pos))[None, :, None, :, None]
    t_chunk = jnp.einsum('bhnjd,bhnjv->nbhdv', k_dec, v)
    g_c = jnp.exp(log_gamma * c)[None, :, None, None]

    def step(r, t_n):
        return g_c * r + t_n, r

    _, r_prev = lax.scan(step, jnp.zeros_like(t_chunk[0]), t_chunk)
    q_dec = q * jnp.exp(lg * (pos + 1.0))[None, :, None, :, None]
    cross = jnp.einsum('bhnid,nbhdv->bhniv', q_dec, r_prev)
    return intra + cross

def retention_mixer(q, k, v, g, gn_w):
    qf = rotary(heads(q, H_RET).astype(jnp.float32))
    kf = rotary(heads(k, H_RET).astype(jnp.float32)) * (DK_RET ** -0.5)
    vf = heads(v, H_RET).astype(jnp.float32)
    log_gamma = jnp.log(1.0 - jnp.power(2.0, -5.0 - jnp.arange(H_RET, dtype=jnp.float32)))

    def run(qq, kk, vv, strict):
        return from_chunks(retention_dir(to_chunks(qq, RET_CHUNK), to_chunks(kk, RET_CHUNK),
                                         to_chunks(vv, RET_CHUNK), log_gamma, strict))

    y = run(qf, kf, vf, False) + flip_seq(run(flip_seq(qf), flip_seq(kf), flip_seq(vf), True))
    out = head_layer_norm(y, gn_w) * jax.nn.silu(g.astype(jnp.float32))
    return out.astype(q.dtype)

def gated_chunk_dir(q, k, v, logf):
    c = q.shape[3]
    causal = jnp.tril(jnp.ones((c, c), dtype=bool))

    def step(s, inp):
        qc, kc, vc, lfc = inp
        b = jnp.cumsum(lfc, axis=2)
        diff = b[:, :, :, None, :] - b[:, :, None, :, :]
        w = jnp.where(causal[:, :, None], jnp.exp(jnp.minimum(diff, 0.0)), 0.0)
        a = jnp.einsum('bhijd,bhjd->bhij', w * qc[:, :, :, None, :], kc)
        intra = jnp.einsum('bhij,bhjv->bhiv', a, vc)
        inter = jnp.einsum('bhid,bhdv->bhiv', qc * jnp.exp(b), s)
        b_last = b[:, :, -1:, :]
        s_new = jnp.exp(b_last[:, :, 0, :])[..., None] * s + jnp.einsum('bhjd,bhjv->bhdv', kc * jnp.exp(b_last - b), vc)
        return s_new, intra + inter

    mv = lambda t: jnp.moveaxis(t, 2, 0)
    bsz, h = q.shape[0], q.shape[1]
    s0 = jnp.zeros((bsz, h, q.shape[-1], v.shape[-1]), jnp.float32)
    _, o = lax.scan(step, s0, (mv(q), mv(k), mv(v), mv(logf)))
    return jnp.moveaxis(o, 0, 2)

def hgrn2_mixer(q, i, zf_fwd, zf_bwd, g, lb, gn_w):
    qf = heads(q, H_HG).astype(jnp.float32)
    inp = heads(i, H_HG).astype(jnp.float32)
    lbh = lb.reshape(H_HG, DK_HG)

    def log_forget(z):
        zf = heads(z, H_HG).astype(jnp.float32)
        return jnp.logaddexp(jnp.log(lbh), jnp.log1p(-lbh) + jax.nn.log_sigmoid(zf))

    def run(qq, ii, lf):
        kk = -jnp.expm1(lf)
        o = gated_chunk_dir(to_chunks(qq, HG_CHUNK), to_chunks(kk, HG_CHUNK),
                            to_chunks(ii, HG_CHUNK), to_chunks(lf, HG_CHUNK))
        return from_chunks(o)

    y = run(qf, inp, log_forget(zf_fwd)) + flip_seq(run(flip_seq(qf), flip_seq(inp), flip_seq(log_forget(zf_bwd))))
    out = head_rms_norm(y, gn_w) * jax.nn.silu(g.astype(jnp.float32))
    return out.astype(q.dtype)

def expert_choice_ffn(h, w_router, w_gate, w_up, w_down):
    bsz, s, d = h.shape
    t = h.reshape(bsz * s, d)
    n_tok = bsz * s
    cap = CAPACITY_FACTOR * n_tok // N_EXPERTS
    aff = jax.nn.softmax((t @ w_router).astype(jnp.float32), axis=-1)
    gate, idx = lax.top_k(aff.T, cap)
    xe = t[idx]
    a = jnp.einsum('ecd,edf->ecf', xe, w_gate)
    u = jnp.einsum('ecd,edf->ecf', xe, w_up)
    ye = jnp.einsum('ecf,efd->ecd', jax.nn.silu(a) * u, w_down)
    ye = ye * gate[..., None].astype(ye.dtype)
    out = jnp.zeros_like(t).at[idx.reshape(-1)].add(ye.reshape(-1, d))
    return out.reshape(bsz, s, d)

def encoder_layer(x, c, w_ada, b_ada, g_pre1, g_post1, w_in, gn_ret, gn_hg, lb, w_br_ret, w_br_hg,
                  w_out, g_pre2, g_post2, w_router, w_gate, w_up, w_down):
    mod = jax.nn.silu(c) @ w_ada + b_ada
    sh1, sc1, ga1, sh2, sc2, ga2 = jnp.split(mod[:, None, :], 6, axis=-1)
    h = rms_norm(x, g_pre1) * (1.0 + sc1) + sh1
    u = h @ w_in
    qr, kr, vr, gr, qh, ih, ffh, fbh, gh, za, zb = split_cols(u)
    y_ret = retention_mixer(qr, kr, vr, gr, gn_ret)
    y_hg = hgrn2_mixer(qh, ih, ffh, fbh, gh, lb, gn_hg)
    merged = jax.nn.sigmoid(za) * (y_ret @ w_br_ret) + jax.nn.sigmoid(zb) * (y_hg @ w_br_hg)
    x = x + ga1 * rms_norm(merged @ w_out, g_post1)
    h2 = rms_norm(x, g_pre2) * (1.0 + sc2) + sh2
    x = x + ga2 * rms_norm(expert_choice_ffn(h2, w_router, w_gate, w_up, w_down), g_post2)
    return x

def setup_inputs(seed: int = 0) -> dict:
    key = jax.random.key(seed)
    ks = jax.random.split(key, 24)
    nrm = lambda k, shape, scale: jax.random.normal(k, shape, jnp.float32) * scale
    gain = lambda k, shape: 1.0 + 0.01 * jax.random.normal(k, shape, jnp.float32)
    L, D = DEPTH, D_MODEL
    return {
        "x_prompt": nrm(ks[0], (BATCH, SEQ, D), 1.0),
        "x_sample": nrm(ks[1], (DEC_BATCH, DEC_SEQ, D), 1.0),
        "c_prompt": nrm(ks[2], (BATCH, D), 1.0),
        "c_sample": nrm(ks[3], (DEC_BATCH, D), 1.0),
        "w_ada": nrm(ks[4], (L, D, 6 * D), 0.5 * D ** -0.5),
        "b_ada": nrm(ks[5], (L, 6 * D), 0.01),
        "g_pre1": gain(ks[6], (L, D)),
        "g_post1": gain(ks[7], (L, D)),
        "w_in": nrm(ks[8], (L, D, D_IN), D ** -0.5),
        "gn_ret": gain(ks[9], (L, RET_V)),
        "gn_hg": gain(ks[10], (L, HG_V)),
        "lb_logits": nrm(ks[11], (L + 1, HG_K), 0.5),
        "w_br_ret": nrm(ks[12], (L, RET_V, D), RET_V ** -0.5),
        "w_br_hg": nrm(ks[13], (L, HG_V, D), HG_V ** -0.5),
        "w_out": nrm(ks[14], (L, D, D), D ** -0.5),
        "g_pre2": gain(ks[15], (L, D)),
        "g_post2": gain(ks[16], (L, D)),
        "w_router": nrm(ks[17], (L, D, N_EXPERTS), D ** -0.5),
        "w_gate": nrm(ks[18], (L, N_EXPERTS, D, D_EXPERT), D ** -0.5),
        "w_up": nrm(ks[19], (L, N_EXPERTS, D, D_EXPERT), D ** -0.5),
        "w_down": nrm(ks[20], (L, N_EXPERTS, D_EXPERT, D), D_EXPERT ** -0.5),
    }

def reference(x_prompt, x_sample, c_prompt, c_sample, w_ada, b_ada, g_pre1, g_post1, w_in, gn_ret, gn_hg,
              lb_logits, w_br_ret, w_br_hg, w_out, g_pre2, g_post2, w_router, w_gate, w_up, w_down):
    lower_bounds = jnp.cumsum(jax.nn.softmax(lb_logits.astype(jnp.float32), axis=0), axis=0)
    xp, xs = x_prompt, x_sample
    for l in range(DEPTH):
        params = (w_ada[l], b_ada[l], g_pre1[l], g_post1[l], w_in[l], gn_ret[l], gn_hg[l], lower_bounds[l],
                  w_br_ret[l], w_br_hg[l], w_out[l], g_pre2[l], g_post2[l], w_router[l], w_gate[l], w_up[l], w_down[l])
        xp = encoder_layer(xp, c_prompt, *params)
        xs = encoder_layer(xs, c_sample, *params)
    return (xp, xs)


_drawn_inputs = setup_inputs


def setup_inputs(seed=0):
    import zlib

    import numpy as np

    out = dict(_drawn_inputs(seed))
    spreads = {}
    factors = {'g_pre1': 2.843,
     'g_post1': 3.163,
     'gn_ret': 6.272,
     'gn_hg': 5.029,
     'g_pre2': 2.682,
     'g_post2': 8.0}
    for name, (base, spread) in spreads.items():
        noise = np.random.default_rng([zlib.crc32(name.encode()), seed]).standard_normal(out[name].shape)
        drawn = base * np.exp(spread * noise) if base else spread * noise
        out[name] = __import__('jax').numpy.asarray(drawn.astype(out[name].dtype))
    for name, factor in factors.items():
        out[name] = (out[name] * factor).astype(out[name].dtype)
    return out
```

```python
from contextlib import ExitStack

import numpy as np

import concourse.bass as bass
from concourse import mybir

F32 = mybir.dt.float32
F32R = mybir.dt.float32r
U32 = mybir.dt.uint32
U8 = mybir.dt.uint8
ALU = mybir.AluOpType
ACT = mybir.ActivationFunctionType
AX_X = mybir.AxisListType.X

P = 128
D = 1024
KC = D // P
SEQS = (256, 1024)
NTOK = sum(SEQS)
NT = NTOK // P
TILE_GROUP = [0 if t < SEQS[0] // P else 1 for t in range(NT)]
FIRST_TILE = [TILE_GROUP.index(g) for g in range(2)]
LAST_TILE = [NT - 1 - TILE_GROUP[::-1].index(g) for g in range(2)]
HEADS = 4
NCOLG = 9
QR, KR, VR, GR, QH, IH, FF, FB, GH = range(NCOLG)
LEVELS = (64, 32, 16, 8, 4)
EPS = 1e-6
HIGH_BITS = 0xFFFFF000
LOG_FORGET_MIN = -20.0
NE = 16
DE = 2048
CAPS = tuple(2 * s // NE for s in SEQS)
CAPT = sum(CAPS)
BLKS = [(0, 512), (512, 512), (1024, 256)]
TGRP = [(0, 4), (4, 4), (8, 2)]


def shape_constants():
    f = np.float32
    half = 64
    inv = (f(1.0) / (f(10000.0) ** (np.arange(half, dtype=f) / f(half)))).astype(f)
    ang = np.arange(SEQS[1], dtype=f)[:, None] * inv[None, :]
    cs = np.stack([np.cos(ang), np.sin(ang)], 1).astype(f)
    rot = cs.reshape(SEQS[1] // P, P, 2, half).transpose(1, 0, 2, 3)
    pos = np.arange(P, dtype=np.float64)
    ret = np.zeros((HEADS, P, 388), f)
    for h in range(HEADS):
        gam = 1.0 - 2.0 ** (-5.0 - h)
        ret[h, :, 0:128] = gam ** np.abs(pos[:, None] - pos[None, :]) * 128 ** -0.5
        ret[h, :, 128:256] = gam ** (pos + 1)
        ret[h, :, 256:384] = gam ** (P - pos)
        ret[h, :, 384] = gam ** (P - 1 - pos) * 128 ** -0.5
        ret[h, :, 385] = gam ** pos * 128 ** -0.5
        ret[h, :, 386] = gam ** P
    j, i = np.meshgrid(np.arange(P), np.arange(P), indexing="ij")
    masks = []
    for m in LEVELS:
        same, jh, ih = j // (2 * m) == i // (2 * m), (j // m) % 2, (i // m) % 2
        masks += [same & (jh == 0) & (ih == 1), same & (jh == 1) & (ih == 0)]
    leaf = j // 4 == i // 4
    leaves = np.stack([leaf & (j <= i), leaf & (j >= i)], 1).astype(f)
    return {
        "ident": np.eye(P, dtype=f),
        "flip": np.ascontiguousarray(np.eye(P, dtype=f)[::-1]),
        "rot": np.ascontiguousarray(rot),
        "ret": ret,
        "masks": np.ascontiguousarray(np.stack(masks, 1).astype(f)),
        "leaves": np.ascontiguousarray(leaves),
    }


def phase_modulation(nc, t):
    with ExitStack() as ctx:
        sb = lambda n, s, d=F32: ctx.enter_context(nc.sbuf_tensor(n, s, d))
        sem = lambda n: ctx.enter_context(nc.semaphore("m_" + n))
        W = 256
        PER = D // W
        NJ = 6 * PER
        ORDER = (0, 1, 2, 5, 3, 4)
        NW = 4
        NX = NT // 2
        COLS1 = 2 * PER
        SQUARES, NORM = 6, 7
        TURN = 11
        x_sb = sb("x_sb", [P, NT, D])
        square = sb("square", [P, 2 * len(LEVELS) * P])
        ssum = sb("ssum", [P, NT])
        c_raw = sb("c_raw", [P, KC, 2])
        c_silu = sb("c_silu", [P, KC, 2])
        w_ring = sb("w_ring", [P, NW, KC, W])
        mod = sb("mod", [2, 6 * D])
        post = sb("post", [2, 2, D])
        gate_rows = sb("gate_rows", [2, 2, D])
        pre_cols = sb("pre_cols", [P, 2, KC])
        lb_cols = sb("lb_cols", [P, 2, HEADS])
        lb_diff = sb("lb_diff", [P, HEADS])
        lb_low = sb("lb_low", [P, HEADS])
        gn_cols = sb("gn_cols", [P, 2, HEADS])
        ps_mod = [ctx.enter_context(nc.psum_tensor(f"ps_mod{i}", [P, 512], F32)) for i in range(2)]
        ps_col = ctx.enter_context(nc.psum_tensor("ps_col", [P, 512], F32))
        ps_x = [ctx.enter_context(nc.psum_tensor(f"ps_x{i}", [P, 512], F32)) for i in range(4)]
        s_c, s_bias, s_small, s_masks = sem("c"), sem("bias"), sem("small"), sem("masks")
        s_w = [sem(f"w{i}") for i in range(NW)]
        s_x = [sem(f"x{i}") for i in range(NX)]
        s_csilu, s_mod, s_modsb, s_col = sem("csilu"), sem("mod"), sem("modsb"), sem("col")
        s_cols, s_ss, s_var, s_rstd, s_xn = sem("cols"), sem("ss"), sem("var"), sem("rstd"), sem("xn")
        s_xt, s_xact, s_xdve = sem("xt"), sem("xact"), sem("xdve")
        s_rows, s_lb, s_gstore, s_head = sem("rows"), sem("lb"), sem("gstore"), sem("head")
        NSMALL = 9
        w_ada = t.w_ada[0].rearrange("(p k) n -> p k n", k=KC)
        w_in = t.w_in[0][:, 0:NCOLG * HEADS * P].rearrange("(c p) (g h x) -> c p h g x", p=P, g=NCOLG, h=HEADS)

        def columns_of(j):
            o = ORDER[j // PER] * D + j % PER * W
            return slice(o, o + W)

        def evacuate(eng, u):
            tl, hf = divmod(u, 2)
            g = TILE_GROUP[tl]
            eng.wait_ge(s_xt, u + 1)
            for c in range(4):
                cc = 4 * hf + c
                dst, src = t.hT[:, cc, tl * P:(tl + 1) * P], ps_x[u % 4][:, c * P:(c + 1) * P]
                a, b = t.scale1[:, cc, g:g + 1], t.shift1[:, cc, g:g + 1]
                if u % 2 == 0:
                    ins = eng.activation(dst, src, ACT.Identity, scale=a, bias=b)
                else:
                    ins = eng.tensor_scalar(dst, src, a, b, ALU.mult, ALU.add)
            ins.then_inc(s_xact if u % 2 == 0 else s_xdve, 1)

        block = ctx.enter_context(nc.Block())

        @block.sync
        def _(sp):
            def load_w(j):
                if j >= NW:
                    sp.wait_ge(s_mod, j - NW + 1)
                sp.dma_start(w_ring[:, j % NW], w_ada[:, :, columns_of(j)]).then_inc(s_w[j % NW], 16)

            with nc.allow_non_contiguous_dma(reason="vectors into columns, once"):
                for g, c in enumerate((t.c_prompt, t.c_sample)):
                    sp.dma_start(c_raw[:, :, g], c[0].rearrange("(p k) -> p k", k=KC)).then_inc(s_c, 16)
                load_w(0)
                load_w(1)
                sp.dma_start(mod[:], t.b_ada.to_broadcast([2, 6 * D])).then_inc(s_bias, 16)
                load_w(2)
                load_w(3)
                sp.dma_start(t.ident[:], t.c_ident).then_inc(s_small, 16)
                for n, v in enumerate((t.g_pre1, t.g_pre2)):
                    sp.dma_start(pre_cols[:, n], v[0].rearrange("(c p) -> p c", p=P)).then_inc(s_small, 16)
                for n, v in enumerate((t.g_post1, t.g_post2)):
                    sp.dma_start(post[:, n], v.to_broadcast([2, D])).then_inc(s_small, 16)
                for n in range(2):
                    sp.dma_start(lb_cols[:, n], t.lb_logits[n].rearrange("(h p) -> p h", p=P)).then_inc(s_small, 16)
                for n, v in enumerate((t.gn_ret, t.gn_hg)):
                    sp.dma_start(gn_cols[:, n], v[0].rearrange("(h p) -> p h", p=P)).then_inc(s_small, 16)
            for j in range(NW, NJ):
                load_w(j)
                i = (j - NW) // 2
                if (j - NW) % 2 == 0 and i < NX:
                    g = TILE_GROUP[2 * i]
                    rows = (t.x_prompt, t.x_sample)[g][0].rearrange("(t p) d -> p t d", p=P)
                    o = 2 * i - FIRST_TILE[g]
                    sp.dma_start(x_sb[:, 2 * i:2 * i + 2], rows[:, o:o + 2]).then_inc(s_x[i], 16)
                c = j - (NW + 2 * NX)
                if 0 <= c < KC:
                    sp.dma_start(t.w_head[:, c], w_in[c][:, 0]).then_inc(s_head, 16)
            sp.wait_ge(s_rows, 2)
            for v in range(2):
                sp.dma_start(t.gates_dram[v], gate_rows[:, v]).then_inc(s_gstore, 16)
            for c in range(NJ - NW - 2 * NX, KC):
                sp.dma_start(t.w_head[:, c], w_in[c][:, 0]).then_inc(s_head, 16)
            sp.dma_start(t.rot[:], t.c_rot).then_inc(s_head, 16)
            sp.dma_start(t.leaves[:], t.c_leaves).then_inc(s_head, 16)
            sp.wait_ge(s_ss, NT)
            sp.dma_start(square[:].rearrange("p (m x) -> p m x", x=P), t.c_masks).then_inc(s_masks, 16)
            sp.wait_ge(s_gstore, 32)
            sp.wait_ge(s_head, 16 * (KC + 2))

        @block.tensor
        def _(pe):
            def mod_rows(j):
                pe.wait_ge(s_w[j % NW], 16 * (j // NW + 1))
                if j >= 2:
                    pe.wait_ge(s_modsb, j - 1)
                for k in range(KC):
                    mm = pe.matmul(ps_mod[j % 2][0:2, 0:W], c_silu[:, k, :], w_ring[:, j % NW, k, :],
                                   start=(k == 0), stop=(k == KC - 1))
                mm.then_inc(s_mod, 1)

            def columns(vectors):
                for v, src in vectors:
                    for c in range(KC):
                        o = 16 * v + 2 * c
                        mm = pe.transpose(ps_col[:, o:o + 2], mod[:, src * D + c * P:src * D + (c + 1) * P],
                                          t.ident[0:2, 0:2])
                mm.then_inc(s_col, 1)

            def turn(u):
                tl, hf = divmod(u, 2)
                pe.wait_ge(s_xn, tl + 1)
                if u >= 4:
                    pe.wait_ge(s_xact if u % 2 == 0 else s_xdve, (u - 4) // 2 + 1)
                for c in range(4):
                    cc = 4 * hf + c
                    mm = pe.transpose(ps_x[u % 4][:, c * P:(c + 1) * P], x_sb[:, tl, cc * P:(cc + 1) * P], t.ident[:])
                mm.then_inc(s_xt, 1)

            pe.wait_ge(s_csilu, 1)
            for j in range(NJ):
                mod_rows(j)
                if j == COLS1:
                    pe.wait_ge(s_small, 16 * NSMALL)
                    pe.wait_ge(s_modsb, COLS1)
                    columns([(0, 0), (1, 1)])
                if TURN <= j < TURN + NT:
                    turn(2 * (j - TURN))
                    turn(2 * (j - TURN) + 1)
            pe.wait_ge(s_modsb, NJ)
            columns([(2, 3), (3, 4)])

        @block.scalar
        def _(act):
            act.wait_ge(s_c, 32)
            act.activation(c_silu[:], c_raw[:], ACT.Silu).then_inc(s_csilu, 1)
            act.wait_ge(s_lb, 1)
            act.activation(lb_low[:], lb_diff[:], ACT.Sigmoid).then_inc(s_lb, 1)
            for j in range(NJ):
                i = (j - SQUARES) // 2
                if (j - SQUARES) % 2 == 0 and 0 <= i < NX:
                    act.wait_ge(s_x[i], 16)
                    for tl in (2 * i, 2 * i + 1):
                        act.drain()
                        act.activation(square[:, 0:D], x_sb[:, tl], ACT.Square,
                                       accum_out=ssum[:, tl:tl + 1]).then_inc(s_ss, 1)
                i = (j - NORM) // 2
                if (j - NORM) % 2 == 0 and 0 <= i < NX:
                    act.wait_ge(s_var, i + 1)
                    act.activation(ssum[:, 2 * i:2 * i + 2], ssum[:, 2 * i:2 * i + 2], ACT.Sqrt).then_inc(s_rstd, 1)
                if j == TURN:
                    act.wait_ge(s_cols, 1)
                if TURN <= j < TURN + NT:
                    evacuate(act, 2 * (j - TURN))

        @block.gpsimd
        def _(pool):
            for tl in range(1, NT, 2):
                pool.wait_ge(s_rstd, tl // 2 + 1)
                pool.tensor_scalar(x_sb[:, tl], x_sb[:, tl], ssum[:, tl:tl + 1], None, ALU.mult)
                pool.drain()
                pool.wait_ge(s_xn, tl)
                pool.sem_inc(s_xn, 1)

        @block.vector
        def _(dve):
            def head_columns():
                dve.wait_ge(s_lb, 2)
                dve.tensor_copy(t.head_cols[:, :, 0], lb_low[:])
                dve.tensor_scalar(t.head_cols[:, :, 1], lb_low[:], -1.0, 1.0, ALU.mult, ALU.add)
                dve.tensor_copy(t.head_cols[:, :, 2], gn_cols[:, 0])
                dve.tensor_copy(t.head_cols[:, :, 3], gn_cols[:, 1])

            def rows(j):
                dve.wait_ge(s_mod, j + 1)
                sl = columns_of(j)
                dve.tensor_tensor(mod[:, sl], ps_mod[j % 2][0:2, 0:W], mod[:, sl], ALU.add).then_inc(s_modsb, 1)

            def scale_shift(n, scale, shift, v):
                dve.wait_ge(s_col, n + 1)
                sh = ps_col[:, 16 * v:16 * v + 16].rearrange("p (c g) -> p c g", g=2)
                sc = ps_col[:, 16 * v + 16:16 * v + 32].rearrange("p (c g) -> p c g", g=2)
                dve.tensor_copy(shift, sh)
                dve.scalar_tensor_tensor(out=scale, in0=sc, scalar=1.0,
                                         in1=pre_cols[:, n].unsqueeze(2).to_broadcast([P, KC, 2]),
                                         op0=ALU.add, op1=ALU.mult)
                dve.drain()
                dve.sem_inc(s_cols, 1)

            def gate_row(n, v):
                dve.drain()
                dve.tensor_tensor(gate_rows[:, n], mod[:, v * D:(v + 1) * D], post[:, n], ALU.mult).then_inc(s_rows, 1)

            def norm(i):
                v = ssum[:, 2 * i:2 * i + 2]
                dve.wait_ge(s_ss, 2 * i + 2)
                dve.tensor_scalar(v, v, 1.0 / D, EPS, ALU.mult, ALU.add)
                dve.drain()
                dve.reciprocal(v, v).then_inc(s_var, 1)
                dve.wait_ge(s_rstd, i + 1)
                dve.tensor_scalar(x_sb[:, 2 * i], x_sb[:, 2 * i], ssum[:, 2 * i:2 * i + 1], None, ALU.mult)
                dve.drain()
                if i >= 1:
                    dve.wait_ge(s_xn, 2 * i)
                dve.sem_inc(s_xn, 1)

            dve.memset(t.ones[:], 1.0)
            dve.wait_ge(s_bias, 16)
            dve.wait_ge(s_small, 16 * NSMALL)
            dve.tensor_sub(lb_diff[:], lb_cols[:, 0], lb_cols[:, 1]).then_inc(s_lb, 1)
            for j in range(NJ):
                rows(j)
                if j == 1:
                    head_columns()
                if j == COLS1:
                    scale_shift(0, t.scale1[:], t.shift1[:], 0)
                i = (j - NORM) // 2
                if (j - NORM) % 2 == 0 and 0 <= i < NX:
                    norm(i)
                if j in (3 * PER - 1, 4 * PER - 1):
                    gate_row(j // PER - 2, ORDER[j // PER])
                if TURN <= j < TURN + NT:
                    evacuate(dve, 2 * (j - TURN) + 1)
            scale_shift(1, t.scale2[:], t.shift2[:], 2)
            dve.wait_ge(s_masks, 16)
            dve.tensor_copy(t.masks[:], square[:].rearrange("p (m x) -> p m x", x=P))


def phase_heads(nc, t):
    with ExitStack() as ctx:
        sb = lambda n, s, d=F32: ctx.enter_context(nc.sbuf_tensor(n, s, d))
        psum = lambda n: ctx.enter_context(nc.psum_tensor(n, [P, 512], F32))
        names = []

        def sem(n):
            names.append(ctx.enter_context(nc.semaphore("h_" + n)))
            return names[-1]

        w, rot, masks, leaves, ones = t.w_head, t.rot, t.masks, t.leaves, t.ones
        ret_c = sb("ret_c", [P, 388])
        cols = sb("cols", [P, 4])
        logf = sb("logf", [P, 2, NT, 129])
        keyT = sb("keyT", [P, 2, NTOK])
        qT = sb("qT", [P, NTOK])
        qdT = sb("qdT", [P, 2, NTOK])
        val = sb("val", [P, NT, P])
        fac = sb("fac", [P, 3, NTOK])
        fac2 = sb("fac2", [P, NTOK])
        key_dec = sb("key_dec", [P, 2, NT, P])
        probs = sb("probs", [P, NT, P])
        tmp = sb("tmp", [P, 512])
        state = logf[:, :, :, 0:P]
        tile_decay = sb("tile_decay", [P, 2, NT])
        gated = sb("gated", [P, 2, NTOK])
        rval = sb("rval", [P, NT, P])
        rk_dec = sb("rk_dec", [P, 2, NT, P])
        qk = sb("qk", [P, 2, 2, P])
        m12 = sb("m12", [P, 2, 2, 256])
        rqT = sb("rqT", [P, NTOK])
        rkT = sb("rkT", [P, NTOK])
        rprobs = fac[:, 2].rearrange("p (t x) -> p t x", x=P)
        rstate = fac[:, 0:2].rearrange("p d (t x) -> p d t x", x=P)
        rqdT = key_dec[:].rearrange("p d t x -> p d (t x)")
        ysb = keyT[:].rearrange("p d (t x) -> p d t x", x=P)
        stats = sb("stats", [P, 2 * NT, 6])
        mv = sb("mv", [P, 2, NT, 2])
        rstd = sb("rstd_h", [P, 2, NT])
        ps_a = [psum(f"ps_a{i}") for i in range(2)]
        NS = 4
        ps_s = [psum(f"ps_s{i}") for i in range(NS)]
        ps_t = [psum(f"ps_t{i}") for i in range(2)]

        s_in = sem("in")
        s_next = sem("next")
        s_store = ctx.enter_context(nc.semaphore("h_store"))
        s_a = sem("a")
        s_aact, s_advec = sem("aact"), sem("adve")
        s_sig = sem("sig")
        s_ln = sem("ln")
        s_lnc = sem("lnc")
        s_keys = sem("keys")
        s_q = sem("q")
        s_sub, s_exp, s_mul = sem("sub"), sem("exp"), sem("mul")
        s_s, s_sfree = sem("s"), sem("sfree")
        s_item = sem("item")
        s_t = sem("t")
        s_tact, s_tdve = sem("tact"), sem("tdve")
        s_rm, s_rot, s_kd = sem("rm"), sem("rot"), sem("kd")
        s_tiles = sem("tiles")
        s_prob, s_state, s_y, s_ycopy = sem("prob"), sem("state"), sem("y"), sem("ycopy")
        s_rec, s_sqrt, s_norm, s_out = sem("rec"), sem("sqrt"), sem("norm"), sem("out")
        s_yt = sem("yt")
        s_cols = sem("cols")
        s_rq = sem("rq")

        units = [("ff", b) for b in range(3)] + [("fb", b) for b in range(3)] + [("q", b) for b in range(3)]
        NF = len(units)
        units += [("v", b) for b in range(3)] + [("ret", tl) for tl in range(NT)]
        units += [("g", b) for b in range(3)] + [("rg", b) for b in range(3)]
        act_units = [u for u, (k, _) in enumerate(units) if k != "q"]
        dve_units = [u for u, (k, _) in enumerate(units) if k in ("q", "ret")]
        unit_of = units.index
        levels = [(lv, d) for lv in range(len(LEVELS)) for d in range(2)]
        items = [("key", 0), ("key", 1), ("query", 0), ("query", 1), ("leaf", 0)] + levels[:2]
        items += [("leaf", 1)] + levels[2:]
        NI = len(items)
        def s_units_before(i):
            return 3 * max(0, i - 4)
        SU_HSTATE = 3 * (NI - 4)
        SU_RSCORE = SU_HSTATE + 4
        SU_RSTATE = SU_RSCORE + 3
        SU_Y = [SU_RSTATE + 4, SU_RSTATE + 7]
        state_tiles = {0: [tl for tl in range(NT) if tl not in LAST_TILE],
                       1: [tl for tl in range(NT - 1, -1, -1) if tl not in FIRST_TILE]}
        t_units = [("key0", g, "act") for g in range(3)] + [("key1", g, "act") for g in range(3)]
        t_units += [("qk", tl, "act") for tl in range(NT)]
        t_units += [("y0", g, "dve") for g in range(3)] + [("y1", g, "dve") for g in range(3)]

        def tu(what, n):
            return next(i for i, (a, b, _) in enumerate(t_units) if (a, b) == (what, n))

        def wait_t_free(pe, u):
            if u < 2:
                return
            who = t_units[u - 2][2]
            if who in ("act", "both"):
                pe.wait_ge(s_tact, sum(x[2] in ("act", "both") for x in t_units[:u - 1]))
            if who in ("dve", "both"):
                pe.wait_ge(s_tdve, sum(x[2] in ("dve", "both") for x in t_units[:u - 1]))

        w_next = t.w_in[0][:, P:P + NCOLG * HEADS * P].rearrange(
            "(c p) (g h x) -> c p h g x", p=P, g=NCOLG, h=HEADS)
        yT_dram = t.yT_dram

        def tiles(ap):
            return ap.rearrange("p (t x) -> p t x", x=P)

        with nc.Block() as block:
            @block.sync
            def _(sp):
                sp.sem_inc(s_store, 1)

        with nc.Fori(0, HEADS) as n:
            with nc.Block() as block:
                @block.sync
                def _(sp):
                    sp.dma_start(ret_c[:], t.c_ret[n]).then_inc(s_in, 16)
                    sp.wait_ge(s_a, len(units))
                    for c in range(KC):
                        sp.dma_start(w[:, c], w_next[c][:, n]).then_inc(s_next, 16)
                    for m in range(2):
                        sp.wait_ge(s_out, m + 1)
                        sp.dma_start(yT_dram[m, n], gated[:, 1 - m]).then_inc(s_store, 16)
                    sp.wait_ge(s_next, 16 * KC)

                @block.tensor
                def _(pe):
                    def project(u):
                        kind, b = units[u]
                        if u >= 2:
                            if u - 2 in act_units:
                                pe.wait_ge(s_aact, sum(x <= u - 2 for x in act_units))
                            if u - 2 in dve_units:
                                pe.wait_ge(s_advec, sum(x <= u - 2 for x in dve_units))
                        bank = ps_a[u % 2]
                        if kind in ("ff", "fb", "q", "g", "rg"):
                            g = {"ff": FF, "fb": FB, "q": QH, "g": GH, "rg": GR}[kind]
                            o, m = BLKS[b]
                            for c in range(KC):
                                mm = pe.matmul(bank[:, 0:m], w[:, c, g], t.hT[:, c, o:o + m],
                                               start=(c == 0), stop=(c == KC - 1))
                        elif kind == "v":
                            o, m = TGRP[b]
                            for x in range(m):
                                for c in range(KC):
                                    mm = pe.matmul(bank[:, x * P:(x + 1) * P], t.hT[:, c, (o + x) * P:(o + x + 1) * P],
                                                   w[:, c, IH], start=(c == 0), stop=(c == KC - 1))
                        else:
                            for c in range(KC):
                                mm = pe.matmul(bank[:, 0:3 * P], t.hT[:, c, b * P:(b + 1) * P], w[:, c, QR:VR + 1],
                                               start=(c == 0), stop=(c == KC - 1))
                        mm.then_inc(s_a, 1)

                    def turn(what, g, source):
                        u = tu(what, g)
                        wait_t_free(pe, u)
                        o, m = TGRP[g]
                        for x in range(m):
                            mm = pe.transpose(ps_t[u % 2][:, x * P:(x + 1) * P], source(o + x), t.ident[:])
                        mm.then_inc(s_t, 1)

                    def wait_s_free(su):
                        last = su - NS
                        if last >= SU_Y[0]:
                            pe.wait_ge(s_ycopy, last - SU_Y[0] + 1)
                        elif last >= 0:
                            pe.wait_ge(s_sfree, last + 1)

                    def item(i):
                        kind, d = items[i]
                        if kind == "query":
                            return
                        pe.wait_ge(s_mul, i + 1)
                        a = fac[:, i % 3]
                        if kind == "key":
                            for g in range(3):
                                turn(f"key{d}", g, lambda x: a[:, x * P:(x + 1) * P])
                            return
                        keys, queries = {("leaf", 0): (fac2, a), ("leaf", 1): (a, fac2)}.get((kind, d), (a, a))
                        for g in range(3):
                            su = s_units_before(i) + g
                            wait_s_free(su)
                            o, m = TGRP[g]
                            for x in range(m):
                                sl = slice((o + x) * P, (o + x + 1) * P)
                                mm = pe.matmul(ps_s[su % NS][:, x * P:(x + 1) * P], keys[:, sl], queries[:, sl],
                                               start=True, stop=True)
                            mm.then_inc(s_s, 1)

                    def turn_qk(tl):
                        u = tu("qk", tl)
                        wait_t_free(pe, u)
                        pe.wait_ge(s_rot, tl + 1)
                        for x in range(2):
                            mm = pe.transpose(ps_t[u % 2][:, x * P:(x + 1) * P], qk[:, tl % 2, x], t.ident[:])
                        mm.then_inc(s_t, 1)

                    for u in range(NF):
                        project(u)
                    for i in range(NI):
                        project(NF + i)
                        item(i)
                        if 5 <= i < NT + 5:
                            turn_qk(i - 5)

                    def states(su0, keys, values, tact):
                        pe.wait_ge(s_tact if tact else s_kd, tact or 2 * NT)
                        for k in range(4):
                            su = su0 + k
                            wait_s_free(su)
                            d = k // 2
                            for x, tl in enumerate(state_tiles[d][4 * (k % 2):4 * (k % 2) + 4]):
                                mm = pe.matmul(ps_s[su % NS][:, x * P:(x + 1) * P], keys[:, d, tl], values[:, tl],
                                               start=True, stop=True)
                            mm.then_inc(s_s, 1)

                    states(SU_HSTATE, key_dec, val, 6)
                    project(NF + NI)
                    for g in range(3):
                        su = SU_RSCORE + g
                        wait_s_free(su)
                        if g == 0:
                            pe.wait_ge(s_tact, 6 + NT)
                        o, m = TGRP[g]
                        for x in range(m):
                            sl = slice((o + x) * P, (o + x + 1) * P)
                            mm = pe.matmul(ps_s[su % NS][:, x * P:(x + 1) * P], rkT[:, sl], rqT[:, sl],
                                           start=True, stop=True)
                        mm.then_inc(s_s, 1)
                    states(SU_RSTATE, rk_dec, rval, 0)

                    def outputs(mixer, pr, values, qd, st):
                        for g in range(3):
                            su = SU_Y[mixer] + g
                            wait_s_free(su)
                            o, m = TGRP[g]
                            for x in range(m):
                                tl = o + x
                                sl = slice(tl * P, (tl + 1) * P)
                                ops = [(pr[:, tl], values[:, tl])]
                                if tl not in FIRST_TILE:
                                    ops.append((qd[:, 0, sl], st[:, 0, tl]))
                                if tl not in LAST_TILE:
                                    ops.append((qd[:, 1, sl], st[:, 1, tl]))
                                for k, (lhs, rhs) in enumerate(ops):
                                    mm = pe.matmul(ps_s[su % NS][:, x * P:(x + 1) * P], lhs, rhs,
                                                   start=(k == 0), stop=(k == len(ops) - 1))
                            mm.then_inc(s_y, 1)

                    pe.wait_ge(s_prob, 1)
                    pe.wait_ge(s_state, 1)
                    outputs(0, probs, val, qdT, state)
                    project(NF + NI + 1)
                    project(NF + NI + 2)
                    pe.wait_ge(s_prob, 2)
                    pe.wait_ge(s_rq, 2)
                    pe.wait_ge(s_state, 2)
                    outputs(1, rprobs, rval, rqdT, rstate)
                    for mixer in range(2):
                        pe.wait_ge(s_norm, mixer + 1)
                        for g in range(3):
                            turn(f"y{mixer}", g, lambda x: ysb[:, mixer, x])

                @block.scalar
                def _(act):
                    act.wait_ge(s_cols, 1)
                    for u in range(6):
                        d, b = divmod(u, 3)
                        o, m = BLKS[b]
                        act.wait_ge(s_a, u + 1)
                        act.activation(fac[:, d, o:o + m], ps_a[u % 2][:, 0:m], ACT.Sigmoid)
                        act.activation(keyT[:, d, o:o + m], ps_a[u % 2][:, 0:m], ACT.Sigmoid, scale=-1.0).then_inc(s_aact, 1)
                    act.drain()
                    for d in range(2):
                        act.activation(logf[:, d, :, 1:129], tiles(fac[:, d]), ACT.Ln,
                                       scale=cols[:, 1:2], bias=cols[:, 0:1]).then_inc(s_ln, 1)

                    def values(b):
                        u = unit_of(("v", b))
                        o, m = TGRP[b]
                        act.wait_ge(s_a, u + 1)
                        act.activation(val[:, o:o + m], ps_a[u % 2][:, 0:m * P].rearrange("p (t x) -> p t x", x=P),
                                       ACT.Copy).then_inc(s_aact, 1)

                    def gate(kind, b):
                        u = unit_of((kind, b))
                        o, m = BLKS[b]
                        act.wait_ge(s_a, u + 1)
                        if (kind, b) == ("g", 0):
                            act.wait_ge(s_store, n * 32 + 1)
                        act.activation(gated[:, 1 if kind == "g" else 0, o:o + m], ps_a[u % 2][:, 0:m],
                                       ACT.Copy).then_inc(s_aact, 1)

                    def exps(i):
                        kind, d = items[i]
                        if i >= 3:
                            act.wait_ge(s_item, i - 2)
                        a = fac[:, i % 3]
                        if kind == "key" and d == 1:
                            act.wait_ge(s_sub, 1)
                            act.activation(tiles(a), logf[:, 1, :, 0:128], ACT.Exp).then_inc(s_exp, 1)
                        elif kind == "query" and d == 0:
                            act.activation(tiles(a), logf[:, 0, :, 1:129], ACT.Exp).then_inc(s_exp, 1)
                        else:
                            act.wait_ge(s_sub, i + 1)
                            if kind == "leaf":
                                act.activation(fac2[:], a, ACT.Exp, scale=-1.0)
                                act.drain()
                            act.activation(a, a, ACT.Exp).then_inc(s_exp, 1)

                    def ret_tile(tl):
                        u = unit_of(("ret", tl))
                        act.wait_ge(s_advec, sum(x <= u for x in dve_units))
                        act.activation(rval[:, tl], ps_a[u % 2][:, 2 * P:3 * P], ACT.Copy).then_inc(s_aact, 1)

                    def key_copy(u):
                        d, g = divmod(u, 3)
                        o, m = TGRP[g]
                        act.wait_ge(s_t, u + 1)
                        act.activation(key_dec[:, d, o:o + m], ps_t[u % 2][:, 0:m * P].rearrange(
                            "p (t x) -> p t x", x=P), ACT.Copy).then_inc(s_tact, 1)

                    def ret_keys(tl):
                        act.wait_ge(s_rot, tl + 1)
                        for d in range(2):
                            act.activation(rk_dec[:, d, tl], qk[:, tl % 2, 1], ACT.Identity,
                                           scale=ret_c[:, 384 + d:385 + d]).then_inc(s_kd, 1)

                    def ret_turned(tl):
                        u = tu("qk", tl)
                        act.wait_ge(s_t, u + 1)
                        sl = slice(tl * P, (tl + 1) * P)
                        act.activation(rqT[:, sl], ps_t[u % 2][:, 0:P], ACT.Copy)
                        act.activation(rkT[:, sl], ps_t[u % 2][:, P:2 * P], ACT.Copy).then_inc(s_tact, 1)

                    act.wait_ge(s_in, 16)
                    exps(0)
                    exps(1)
                    act.activation(tile_decay[:], logf[:, :, :, 128], ACT.Exp).then_inc(s_exp, 1)
                    for i in range(NI):
                        if i + 2 < NI:
                            exps(i + 2)
                        kind, b = units[NF + i]
                        if kind == "v":
                            values(b)
                        elif kind == "ret":
                            ret_tile(b)
                        else:
                            gate(kind, b)
                        if i in (0, 1):
                            for g in range(3):
                                key_copy(3 * i + g)
                        if 4 <= i < NT + 4:
                            ret_keys(i - 4)
                        if 6 <= i < NT + 6:
                            ret_turned(i - 6)
                    gate("rg", 0)

                    def copy_outputs(mixer):
                        for g in range(3):
                            su = SU_Y[mixer] + g
                            o, m = TGRP[g]
                            act.wait_ge(s_y, 3 * mixer + g + 1)
                            act.activation(ysb[:, mixer, o:o + m], ps_s[su % NS][:, 0:m * P].rearrange(
                                "p (t x) -> p t x", x=P), ACT.Copy).then_inc(s_ycopy, 1)

                    copy_outputs(0)
                    gate("rg", 1)
                    act.wait_ge(s_rec, 1)
                    act.activation(rstd[:, 0], rstd[:, 0], ACT.Sqrt).then_inc(s_sqrt, 1)
                    gate("rg", 2)
                    act.drain()
                    act.activation(gated[:], gated[:], ACT.Silu).then_inc(s_sig, 1)
                    copy_outputs(1)
                    act.wait_ge(s_rec, 2)
                    act.activation(rstd[:, 1], rstd[:, 1], ACT.Sqrt).then_inc(s_sqrt, 1)

                @block.gpsimd
                def _(pool):
                    pool.wait_ge(s_cols, 1)
                    for d in range(2):
                        pool.wait_ge(s_ln, d + 1)
                        pool.tensor_scalar(logf[:, d, :, 1:129], logf[:, d, :, 1:129], LOG_FORGET_MIN, None,
                                           ALU.max).then_inc(s_lnc, 1)
                        pool.tensor_scalar(keyT[:, d], keyT[:, d], cols[:, 1:2], None, ALU.mult).then_inc(s_keys, 1)
                    for tl in range(NT):
                        pool.wait_ge(s_rm, tl + 1)
                        if tl >= 2:
                            pool.wait_ge(s_kd, 2 * (tl - 1))
                            pool.wait_ge(s_t, tu("qk", tl - 2) + 1)
                        mc, ms = (m12[:, tl % 2, k].rearrange("p (a h x) -> p a h x", a=2, h=2) for k in range(2))
                        o = qk[:, tl % 2].rearrange("p a (h x) -> p a h x", h=2)
                        pool.tensor_tensor(o[:, :, 0], mc[:, :, 0], ms[:, :, 1], ALU.subtract)
                        pool.tensor_tensor(o[:, :, 1], ms[:, :, 0], mc[:, :, 1], ALU.add).then_inc(s_rot, 1)

                @block.vector
                def _(dve):
                    dve.memset(logf[:, :, :, 0:1], 0.0)
                    dve.tensor_copy(cols[:], t.head_cols[:, n])
                    dve.drain()
                    dve.sem_inc(s_cols, 1)
                    for b in range(3):
                        u = 6 + b
                        o, m = BLKS[b]
                        dve.wait_ge(s_a, u + 1)
                        dve.tensor_copy(qT[:, o:o + m], ps_a[u % 2][:, 0:m]).then_inc(s_advec, 1)
                    for d in range(2):
                        dve.wait_ge(s_lnc, d + 1)
                        dve.wait_ge(s_ln, 2)
                        for tl in range(NT):
                            row = logf[:, d, tl, 1:129]
                            dve.tensor_tensor_scan(row, ones[:], row, 0.0, ALU.mult, ALU.add)
                    dve.drain()

                    def halves(ap, m):
                        return ap.rearrange("p t (b h m) -> p t b h m", h=2, m=m)

                    def sub(i):
                        kind, d = items[i]
                        if i >= 3 and kind != "query":
                            dve.wait_ge(s_item, i - 2)
                        a = tiles(fac[:, i % 3])
                        incl, excl = logf[:, d, :, 1:129], logf[:, d, :, 0:128]
                        end = logf[:, d, :, 128:129].to_broadcast([P, NT, P])
                        if kind == "key":
                            if d == 0:
                                dve.tensor_tensor(a, end, incl, ALU.subtract)
                                dve.drain()
                        elif kind == "query":
                            if d == 1:
                                dve.wait_ge(s_item, i - 2)
                                dve.tensor_tensor(a, end, excl, ALU.subtract)
                                dve.drain()
                        elif kind == "leaf":
                            mid = logf[:, d, :, 2:128:4].unsqueeze(3).to_broadcast([P, NT, P // 4, 4])
                            at = (incl if d == 0 else excl).rearrange("p t (b m) -> p t b m", m=4)
                            dve.tensor_tensor(a.rearrange("p t (b m) -> p t b m", m=4), at, mid, ALU.subtract)
                            dve.drain()
                        else:
                            m = LEVELS[kind]
                            mid = logf[:, d, :, m:128:2 * m].unsqueeze(3).to_broadcast([P, NT, P // (2 * m), m])
                            at = halves(incl if d == 0 else excl, m)
                            o = halves(a, m)
                            dve.tensor_tensor(o[:, :, :, 1], at[:, :, :, 1], mid, ALU.subtract)
                            dve.tensor_tensor(o[:, :, :, 0], mid, at[:, :, :, 0], ALU.subtract)
                            dve.drain()
                        dve.sem_inc(s_sub, 1)

                    def mul(i):
                        kind, d = items[i]
                        dve.wait_ge(s_exp, i + 1 + (i >= 2))
                        a = fac[:, i % 3]
                        if kind == "key":
                            dve.wait_ge(s_keys, d + 1)
                            dve.tensor_tensor(a, a, keyT[:, d], ALU.mult)
                        elif kind == "query":
                            dve.tensor_tensor(qdT[:, d], a, qT[:], ALU.mult)
                        elif kind == "leaf":
                            if d == 0:
                                dve.tensor_tensor(a, a, qT[:], ALU.mult)
                                dve.tensor_tensor(fac2[:], fac2[:], keyT[:, 0], ALU.mult)
                            else:
                                dve.tensor_tensor(a, a, keyT[:, 1], ALU.mult)
                                dve.tensor_tensor(fac2[:], fac2[:], qT[:], ALU.mult)
                        else:
                            m = LEVELS[kind]
                            o = halves(tiles(a), m)
                            first, second = (keyT[:, 0], qT[:]) if d == 0 else (qT[:], keyT[:, 1])
                            for hf, x in enumerate((first, second)):
                                dve.tensor_tensor(o[:, :, :, hf], o[:, :, :, hf], halves(tiles(x), m)[:, :, :, hf], ALU.mult)
                        dve.drain()
                        dve.sem_inc(s_mul, 1)

                    def mask(i):
                        kind, d = items[i]
                        if kind == "key":
                            dve.wait_ge(s_t, 3 * (d + 1))
                            dve.sem_inc(s_item, 1)
                            return
                        if kind == "query":
                            dve.sem_inc(s_item, 1)
                            return
                        for g in range(3):
                            su = s_units_before(i) + g
                            o, m = TGRP[g]
                            dve.wait_ge(s_s, su + 1)
                            src = ps_s[su % NS][:, 0:m * P].rearrange("p (t x) -> p t x", x=P)
                            dst = probs[:, o:o + m]
                            if kind == "leaf":
                                msk = leaves[:, d].unsqueeze(1).to_broadcast([P, m, P])
                                if d == 0:
                                    dve.tensor_tensor(dst, src, msk, ALU.mult).then_inc(s_sfree, 1)
                                else:
                                    tv = tmp[:, 0:m * P].rearrange("p (t x) -> p t x", x=P)
                                    dve.tensor_tensor(tv, src, msk, ALU.mult).then_inc(s_sfree, 1)
                                    dve.drain()
                                    dve.tensor_tensor(dst, dst, tv, ALU.add)
                                    dve.drain()
                            else:
                                msk = masks[:, 2 * kind + d].unsqueeze(1).to_broadcast([P, m, P])
                                dve.copy_predicated(dst, msk, src).then_inc(s_sfree, 1)
                        dve.drain()
                        dve.sem_inc(s_item, 1)

                    def rotate(tl):
                        u = unit_of(("ret", tl))
                        dve.wait_ge(s_a, u + 1)
                        if tl >= 2:
                            dve.wait_ge(s_rot, tl - 1)
                        place = tl - FIRST_TILE[TILE_GROUP[tl]]
                        for k in range(2):
                            ins = dve.tensor_tensor(m12[:, tl % 2, k].rearrange("p (a x) -> p a x", a=4),
                                                    ps_a[u % 2][:, 0:256].rearrange("p (a x) -> p a x", a=4),
                                                    rot[:, place, k].unsqueeze(1).to_broadcast([P, 4, 64]), ALU.mult)
                        ins.then_inc(s_advec, 1)
                        dve.drain()
                        dve.sem_inc(s_rm, 1)

                    sub(0)
                    sub(1)
                    for i in range(NI + 1):
                        if i < NI:
                            mul(i)
                        if i >= 1:
                            mask(i - 1)
                        if i + 2 < NI:
                            sub(i + 2)
                        if 3 <= i < NT + 3:
                            rotate(i - 3)
                    dve.drain()
                    dve.sem_inc(s_prob, 1)

                    def chain(su0, st, decay):
                        for k in range(4):
                            d = k // 2
                            su = su0 + k
                            dve.wait_ge(s_s, su + 1)
                            part = state_tiles[d][4 * (k % 2):4 * (k % 2) + 4]
                            for x, tl in enumerate(part):
                                src = ps_s[su % NS][:, x * P:(x + 1) * P]
                                to = tl + 1 if d == 0 else tl - 1
                                if tl in (FIRST_TILE if d == 0 else LAST_TILE):
                                    dve.tensor_copy(st[:, d, to], src)
                                else:
                                    dve.scalar_tensor_tensor(out=st[:, d, to], in0=st[:, d, tl], scalar=decay(d, tl),
                                                             in1=src, op0=ALU.mult, op1=ALU.add)
                                dve.drain()
                            dve.sem_inc(s_sfree, 1)
                        dve.sem_inc(s_state, 1)

                    chain(SU_HSTATE, state, lambda d, tl: tile_decay[:, d, tl:tl + 1])
                    dve.wait_ge(s_tact, 6 + NT)
                    for d in range(2):
                        dve.tensor_tensor(tiles(rqdT[:, d]), tiles(rqT[:]), ret_c[:, P + P * d:2 * P + P * d].unsqueeze(
                            1).to_broadcast([P, NT, P]), ALU.mult).then_inc(s_rq, 1)
                    dve.wait_ge(s_in, 16)
                    for g in range(3):
                        su = SU_RSCORE + g
                        o, m = TGRP[g]
                        dve.wait_ge(s_s, su + 1)
                        src = ps_s[su % NS][:, 0:m * P].rearrange("p (t x) -> p t x", x=P)
                        dve.tensor_tensor(rprobs[:, o:o + m], src, ret_c[:, 0:P].unsqueeze(1).to_broadcast([P, m, P]),
                                          ALU.mult).then_inc(s_sfree, 1)
                    dve.drain()
                    dve.sem_inc(s_prob, 1)
                    chain(SU_RSTATE, rstate, lambda d, tl: ret_c[:, 386:387])

                    def moments(mixer):
                        for g in range(3):
                            dve.wait_ge(s_ycopy, 3 * mixer + g + 1)
                            for tl in range(TGRP[g][0], sum(TGRP[g])):
                                dve.bn_stats(stats[:, mixer * NT + tl], ysb[:, mixer, tl])
                        dve.drain()
                        for tl in range(NT):
                            k = mixer * NT + tl
                            dve.bn_aggr(mv[:, mixer, tl], stats[:, k:k + 1])
                        dve.drain()
                        r = rstd[:, mixer]
                        if mixer == 0:
                            dve.tensor_tensor(r, mv[:, 0, :, 0], mv[:, 0, :, 0], ALU.mult)
                            dve.drain()
                            dve.scalar_tensor_tensor(out=r, in0=r, scalar=EPS, in1=mv[:, 0, :, 1],
                                                     op0=ALU.add, op1=ALU.add)
                        else:
                            dve.tensor_scalar(r, mv[:, 1, :, 1], EPS, None, ALU.add)
                        dve.drain()
                        dve.reciprocal(r, r).then_inc(s_rec, 1)

                    def normalise(mixer):
                        dve.wait_ge(s_sqrt, mixer + 1)
                        for tl in range(NT):
                            y, r = ysb[:, mixer, tl], rstd[:, mixer, tl:tl + 1]
                            if mixer == 0:
                                dve.tensor_scalar(y, y, r, None, ALU.mult)
                            else:
                                dve.tensor_scalar(y, y, mv[:, 1, tl, 0:1], r, ALU.subtract, ALU.mult)
                        dve.drain()
                        dve.sem_inc(s_norm, 1)

                    for mixer in range(2):
                        moments(mixer)
                        normalise(mixer)
                    dve.wait_ge(s_sig, 1)
                    for mixer in range(2):
                        for g in range(3):
                            u = tu(f"y{mixer}", g)
                            o, m = BLKS[g]
                            dve.wait_ge(s_t, u + 1)
                            out = gated[:, 1 - mixer, o:o + m]
                            gain = cols[:, 3:4] if mixer == 0 else cols[:, 2:3]
                            dve.scalar_tensor_tensor(out=out, in0=ps_t[u % 2][:, 0:m], scalar=gain, in1=out,
                                                     op0=ALU.mult, op1=ALU.mult).then_inc(s_tdve, 1)
                        dve.drain()
                        dve.sem_inc(s_out, 1)

            with nc.Block() as block:
                @block.sync
                def _(sp):
                    for s in names:
                        sp.sem_clear(s)

        with nc.Block() as block:
            @block.sync
            def _(sp):
                sp.wait_ge(s_store, 1 + 32 * HEADS)


def split_products(pe, out, w_high, w_low, x_high, x_low, start, stop):
    pe.matmul(out, w_high, x_high, start=start, stop=False)
    pe.matmul(out, w_high, x_low, start=False, stop=False)
    return pe.matmul(out, w_low, x_high, start=False, stop=stop)


def load_branch(sp, t, o, h):
    for m in range(2):
        sp.dma_start(t.w_br[:, h, m], t.w_br_v[m][o]).then_inc(t.s_branch if h == 0 else t.s_branch1, 16)


def phase_branch_gates(nc, t):
    with ExitStack() as ctx:
        sb = lambda n, s, d=F32: ctx.enter_context(nc.sbuf_tensor(n, s, d))
        sem = lambda n: ctx.enter_context(nc.semaphore("z_" + n))
        w_z = sb("w_z", [P, 2, 2, KC, P])
        w_high, w_low = (sb(n, [P, 2, 2, KC, P], F32R) for n in ("w_high", "w_low"))
        h_high, h_low = (sb(n, [P, KC, NTOK], F32R) for n in ("h_high", "h_low"))
        cut = sb("cut", [P, 2, 1024])
        sig = sb("sig", [P, 2, 2, 512])
        ps = [[ctx.enter_context(nc.psum_tensor(f"ps_z{i}{k}", [P, 512], F32)) for k in range(2)] for i in range(2)]
        s_mm, s_sig = sem("mm"), sem("sig")
        s_store = [sem(f"store{i}") for i in range(2)]
        s_cut, s_high, s_low = sem("cut"), sem("high"), sem("low")
        s_w = [sem(f"w{i}") for i in range(2)]
        ZA = NCOLG * HEADS * P
        w_zv = t.w_in[0][:, ZA:ZA + 2 * D].rearrange("(c p) (z o x) -> z o p c x", p=P, z=2, o=KC)
        UN = 6
        PIECES = [("h", 0, 0), ("h", 0, 2), ("w", 0, 0), ("h", 0, 4), ("h", 0, 6), ("w", 0, 1),
                  ("h", 1, 0), ("h", 1, 2), ("h", 1, 4), ("h", 1, 6), ("h", 2, 0), ("h", 2, 4), ("w", 1, 0), ("w", 1, 1)]
        NPC = len(PIECES)

        def piece(k):
            what, n, x = PIECES[k]
            if what == "w":
                return [a[:, n, x] for a in (w_z, w_high, w_low)]
            o, m = BLKS[n]
            c = 1024 // m
            return [a[:, x:x + c, o:o + m] for a in (t.hT, h_high, h_low)]

        def cut_of(k, like):
            return cut[:, k % 2].rearrange("p (a b) -> p a b", b=like.shape[2])

        def cut_and_low(dve, k, count, raw, low):
            if count is not None:
                dve.wait_ge(s_high, count)
            dve.tensor_scalar(cut_of(k, raw).bitcast(U32), raw.bitcast(U32), HIGH_BITS, None,
                              ALU.bitwise_and).then_inc(s_cut, 1)
            dve.drain()
            dve.tensor_tensor(low, raw, cut_of(k, raw), ALU.subtract).then_inc(s_low, 1)

        def done(what, n, x):
            if what == "w":
                return PIECES.index((what, n, x)) + 1
            step = 1024 // BLKS[n][1]
            return PIECES.index((what, n, x // step * step)) + 1

        block = ctx.enter_context(nc.Block())

        @block.sync
        def _(sp):
            def load(o, h):
                for z in range(2):
                    sp.dma_start(w_z[:, h, z], w_zv[z][o]).then_inc(s_w[h], 16)
            load(0, 0)
            load(1, 1)

            def store(i, u):
                o, m = BLKS[u % 3]
                sp.wait_ge(s_sig, i * UN + (u + 1))
                sp.dma_start(t.sig_dram[i * 2 + u // 3][:, :, o:o + m], sig[:, u % 2, :, 0:m]).then_inc(s_store[u % 2], 16)

            load_branch(sp, t, 0, 0)
            sp.wait_ge(s_low, NPC)
            for m in range(2):
                sp.dma_start(t.yT[:, m], t.yT_dram[m].rearrange("h p n -> p h n")).then_inc(t.s_branch, 16)
            with sp.Fori(0, KC // 2 - 1) as i:
                for h in range(2):
                    for b in range(3):
                        store(i, 3 * h + b)
                    sp.wait_ge(s_mm, i * UN + 3 * (h + 1))
                    load(i * 2 + (2 + h), h)
            for u in range(UN):
                store(KC // 2 - 1, u)
            for k in range(2):
                sp.wait_ge(s_store[k], 16 + 16 * (UN // 2) * (KC // 2))

        @block.vector
        def _(dve):
            for k in range(NPC):
                if PIECES[k][0] == "w":
                    dve.wait_ge(s_w[PIECES[k][1]], 32)
                raw, _, low = piece(k)
                cut_and_low(dve, k, k - 1 if k >= 2 else None, raw, low)
            with dve.Fori(0, KC // 2 - 1) as i:
                for h in range(2):
                    dve.wait_ge(s_w[h], i * 32 + 64)
                    for z in range(2):
                        n = NPC + 2 * h + z
                        cut_and_low(dve, n, i * 4 + (n - 1), w_z[:, h, z], w_low[:, h, z])

        @block.scalar
        def _(act):
            for k in range(2):
                act.sem_inc(s_store[k], 16)

            def sigmoids(i, u):
                o, m = BLKS[u % 3]
                act.wait_ge(s_mm, i * UN + (u + 1))
                act.wait_ge(s_store[u % 2], i * 8 * UN + 16 * (u // 2 + 1))
                for z in range(2):
                    ins = act.activation(sig[:, u % 2, z, 0:m], ps[u % 2][z][:, 0:m], ACT.Sigmoid)
                ins.then_inc(s_sig, 1)

            for k in range(NPC):
                raw, high, _ = piece(k)
                act.wait_ge(s_cut, k + 1)
                act.activation(high, cut_of(k, raw), ACT.Copy).then_inc(s_high, 1)
            with act.Fori(0, KC // 2 - 1) as i:
                for h in range(2):
                    for b in range(3):
                        sigmoids(i, 3 * h + b)
                    for z in range(2):
                        n = NPC + 2 * h + z
                        act.wait_ge(s_cut, i * 4 + (n + 1))
                        act.activation(w_high[:, h, z], cut_of(n, w_z[:, h, z]), ACT.Copy).then_inc(s_high, 1)
            for u in range(UN):
                sigmoids(KC // 2 - 1, u)

        @block.tensor
        def _(pe):
            def split_done(pieces):
                pe.wait_ge(s_high, pieces)
                pe.wait_ge(s_low, pieces)

            def unit(i, u, first):
                h, b = divmod(u, 3)
                o, m = BLKS[b]
                if not first or u >= 2:
                    pe.wait_ge(s_sig, i * UN + (u - 1))
                for z in range(2):
                    if first:
                        split_done(done("w", h, z))
                    elif b == 0 and z == 0:
                        split_done(i * 4 + (NPC - 2 + 2 * h))
                    for c in range(KC):
                        if first and h == 0 and z == 0:
                            split_done(done("h", b, c))
                        mm = split_products(pe, ps[u % 2][z][:, 0:m], w_high[:, h, z, c], w_low[:, h, z, c],
                                            h_high[:, c, o:o + m], h_low[:, c, o:o + m], c == 0, c == KC - 1)
                mm.then_inc(s_mm, 1)

            for u in range(UN):
                unit(0, u, True)
            with pe.Fori(1, KC // 2) as i:
                for u in range(UN):
                    unit(i, u, False)


def phase_merge(nc, t):
    with ExitStack() as ctx:
        sb = lambda n, s, d=F32: ctx.enter_context(nc.sbuf_tensor(n, s, d))
        sem = lambda n: ctx.enter_context(nc.semaphore("g_" + n))
        yT, w_br = t.yT, t.w_br
        NR = 3
        sig = sb("sig_g", [P, NR, 2, 512])
        part = sb("part", [P, 2, 2, 512])
        ps = [[ctx.enter_context(nc.psum_tensor(f"ps_g{i}{k}", [P, 512], F32)) for k in range(2)] for i in range(2)]
        s_mm, s_free, s_part, s_add = (sem(n) for n in ("mm", "free", "part", "add"))
        s_sig = [sem(f"sig{i}") for i in range(NR)]
        UN = 6
        block = ctx.enter_context(nc.Block())

        @block.sync
        def _(sp):
            def load_sig(i, u):
                o, m = BLKS[u % 3]
                sp.dma_start(sig[:, u % NR, :, 0:m], t.sig_dram[i * 2 + u // 3][:, :, o:o + m]).then_inc(s_sig[u % NR], 16)

            for b in range(3):
                load_sig(0, b)
            load_branch(sp, t, 1, 1)
            sp.dma_start(t.w_out_sb[:], t.w_out[0].rearrange("(c p) n -> p c n", p=P)).then_inc(t.s_next, 16)
            sp.dma_start(t.gate1[:], t.gates_dram[0].unsqueeze(0).to_broadcast([P, 2, D])).then_inc(t.s_next, 16)
            sp.dma_start(t.w_r[:], t.w_router[0].rearrange("(c p) n -> p c n", p=P)).then_inc(t.s_next, 16)

            def next_sig(i, u):
                sp.wait_ge(s_free, i * UN + (u + 3))
                load_sig(i + (u + 3) // UN, (u + 3) % UN)

            with sp.Fori(0, KC // 2 - 1) as i:
                for h in range(2):
                    for b in range(3):
                        next_sig(i, 3 * h + b)
                    load_branch(sp, t, i * 2 + (2 + h), h)
            for b in range(3):
                next_sig(KC // 2 - 1, b)

        @block.tensor
        def _(pe):
            with pe.Fori(0, KC // 2) as i:
                for h in range(2):
                    if h == 0:
                        pe.wait_ge(t.s_branch, i * 32 + 64)
                    else:
                        pe.wait_ge(t.s_branch1, i * 32 + 32)
                    for b, (o, m) in enumerate(BLKS):
                        u = 3 * h + b
                        pe.wait_ge(s_free, i * UN + (u + 1))
                        for z in range(2):
                            for c in range(HEADS):
                                mm = pe.matmul(ps[u % 2][z][:, 0:m], w_br[:, h, z, c], yT[:, 1 - z, c, o:o + m],
                                               start=(c == 0), stop=(c == HEADS - 1))
                        mm.then_inc(s_mm, 1)

        @block.vector
        def _(dve):
            dve.sem_inc(s_free, 2)
            with dve.Fori(0, KC // 2) as i:
                for u in range(UN):
                    o, m = BLKS[u % 3]
                    dve.wait_ge(s_mm, i * UN + (u + 1))
                    dve.wait_ge(s_sig[u % NR], i * 32 + 16 * (u // NR + 1))
                    dve.wait_ge(s_add, i * UN + (u + 1))
                    for z in range(2):
                        ins = dve.tensor_tensor(part[:, u % 2, z, 0:m], sig[:, u % NR, z, 0:m],
                                                ps[u % 2][z][:, 0:m], ALU.mult)
                    ins.then_inc(s_free, 1)
                    dve.drain()
                    dve.sem_inc(s_part, 1)

        @block.gpsimd
        def _(pool):
            pool.sem_inc(s_add, 2)
            with pool.Fori(0, KC // 2) as i:
                for u in range(UN):
                    o, m = BLKS[u % 3]
                    pool.wait_ge(s_part, i * UN + (u + 1))
                    pool.tensor_tensor(t.mergedT[:, i * 2 + u // 3, o:o + m], part[:, u % 2, 0, 0:m],
                                       part[:, u % 2, 1, 0:m], ALU.add).then_inc(s_add, 1)


def phase_residual(nc, t):
    with ExitStack() as ctx:
        sb = lambda n, s, d=F32: ctx.enter_context(nc.sbuf_tensor(n, s, d))
        sem = lambda n: ctx.enter_context(nc.semaphore("r_" + n))
        psum = lambda n: ctx.enter_context(nc.psum_tensor(n, [P, 512], F32))
        w_out, w_r, gate = t.w_out_sb, t.w_r, t.gate1
        x = sb("x_r", [P, 3, D])
        x1 = sb("x1_r", [P, 3, D])
        normed = sb("normed", [P, 2, D])
        junk = sb("junk", [P, D])
        h2T = sb("h2T", [P, 2, KC, P])
        zero = sb("zero", [P, D])
        ss = sb("ss_r", [P, 2, NT, 2])
        var = sb("var_r", [P, 2, NT])
        std = sb("std_r", [P, 2, NT])
        lgT = sb("lgT", [NE, NTOK])
        affT = sb("affT", [NE, NTOK])
        lg = sb("lg", [P, NT, NE])
        mx = sb("mx", [P, NT])
        ps_o = [[psum(f"ps_o{i}{k}") for k in range(2)] for i in range(2)]
        ps_t = [psum(f"ps_rt{i}") for i in range(2)]
        ps_l = [psum(f"ps_l{i}") for i in range(2)]
        names = ("o", "ss", "var", "std", "scaled", "x1", "ss2", "var2", "std2", "n", "t", "ta", "tv", "l",
                 "lc", "lt", "sm", "exp", "aff", "at", "junk", "zero", "st", "ofree", "done")
        s = {n: sem(n) for n in names}
        s_x = [sem(f"xin{i}") for i in range(3)]
        s_x1d, s_nd = [sem(f"x1d{i}") for i in range(3)], [sem(f"nd{i}") for i in range(2)]
        xs = [t.x_prompt[0], t.x_sample[0]]

        def rows(tl):
            g = TILE_GROUP[tl]
            o = (tl - FIRST_TILE[g]) * P
            return xs[g][o:o + P]

        block = ctx.enter_context(nc.Block())

        @block.sync
        def _(sp):
            for tl in range(2):
                sp.dma_start(x[:, tl], rows(tl)).then_inc(s_x[tl], 16)
            sp.wait_ge(s["zero"], 1)
            sp.dma_start(t.moe_dram.rearrange("(t p) d -> p t d", p=P),
                         zero[:].unsqueeze(1).to_broadcast([P, NT, D])).then_inc(s["st"], 16)
            for tl in range(NT):
                if 2 <= tl + 2 < NT:
                    if tl >= 1:
                        sp.wait_ge(s["x1"], tl)
                    sp.dma_start(x[:, (tl + 2) % 3], rows(tl + 2)).then_inc(s_x[(tl + 2) % 3], 16)
                sp.wait_ge(s["x1"], tl + 1)
                sp.dma_start(t.x1_dram[tl * P:(tl + 1) * P], x1[:, tl % 3]).then_inc(s_x1d[tl % 3], 16)
                sp.wait_ge(s["n"], tl + 1)
                sp.dma_start(t.xn_dram[tl * P:(tl + 1) * P], normed[:, tl % 2]).then_inc(s_nd[tl % 2], 16)
            sp.wait_ge(s["done"], 3)
            sp.dma_start(t.aff_dram, affT[:]).then_inc(s["st"], 16)
            sp.wait_ge(s["st"], 32)
            for k in range(3):
                sp.wait_ge(s_x1d[k], 16 * len(range(k, NT, 3)))
            for k in range(2):
                sp.wait_ge(s_nd[k], 16 * len(range(k, NT, 2)))

        @block.gpsimd
        def _(pool):
            pool.memset(zero[:], 0.0).then_inc(s["zero"], 1)
            for tl in range(NT):
                pool.wait_ge(s["scaled"], tl + 1)
                pool.wait_ge(s_x[tl % 3], 16 * (tl // 3 + 1))
                pool.tensor_tensor(x1[:, tl % 3], x1[:, tl % 3], x[:, tl % 3], ALU.add).then_inc(s["x1"], 1)

        @block.tensor
        def _(pe):
            def out(tl):
                if tl >= 2:
                    pe.wait_ge(s["scaled"], tl - 1)
                for hf in range(2):
                    for c in range(KC):
                        mm = pe.matmul(ps_o[tl % 2][hf][:], t.mergedT[:, c, tl * P:(tl + 1) * P],
                                       w_out[:, c, hf * 512:(hf + 1) * 512], start=(c == 0), stop=(c == KC - 1))
                mm.then_inc(s["o"], 1)

            def turn(tl):
                pe.wait_ge(s["n"], tl + 1)
                for hf in range(2):
                    if tl >= 1:
                        pe.wait_ge(s["ta"] if hf == 0 else s["tv"], tl)
                    for c in range(4):
                        cc = 4 * hf + c
                        mm = pe.transpose(ps_t[hf][:, c * P:(c + 1) * P], normed[:, tl % 2, cc * P:(cc + 1) * P], t.ident[:])
                    mm.then_inc(s["t"], 1)

            def route(tl):
                pe.wait_ge(s["ta"], tl + 1)
                pe.wait_ge(s["tv"], tl + 1)
                if tl >= 2:
                    pe.wait_ge(s["lc"], tl - 1)
                for c in range(KC):
                    mm = pe.matmul(ps_l[tl % 2][0:NE, 0:P], w_r[:, c], h2T[:, tl % 2, c], start=(c == 0), stop=(c == KC - 1))
                mm.then_inc(s["l"], 1)

            pe.wait_ge(t.s_next, 48)
            for k in range(NT + 3):
                if k < NT:
                    out(k)
                if 2 <= k < NT + 2:
                    turn(k - 2)
                if k >= 3:
                    route(k - 3)
            pe.wait_ge(s["lc"], NT)
            for tl in range(NT):
                mm = pe.transpose(ps_l[0][:, tl * NE:(tl + 1) * NE], lgT[:, tl * P:(tl + 1) * P], t.ident[0:NE, 0:NE])
            mm.then_inc(s["lt"], 1)
            pe.wait_ge(s["aff"], 1)
            for g, (o, m) in enumerate(TGRP):
                bank = [ps_o[0][0], ps_o[0][1], ps_o[1][0]][g]
                for k in range(m):
                    mm = pe.transpose(bank[0:NE, k * P:(k + 1) * P], lg[:, o + k], t.ident[:])
                mm.then_inc(s["at"], 1)

        @block.scalar
        def _(act):
            def squares(tl):
                act.wait_ge(s["o"], tl + 1)
                for hf in range(2):
                    ins = act.activation(junk[:, hf * 512:(hf + 1) * 512], ps_o[tl % 2][hf][:], ACT.Square,
                                         accum_out=ss[:, 0, tl, hf:hf + 1])
                ins.then_inc(s["ss"], 1)
                act.wait_ge(s["var"], tl + 1)
                act.activation(std[:, 0, tl:tl + 1], var[:, 0, tl:tl + 1], ACT.Sqrt).then_inc(s["std"], 1)

            def norm(tl):
                act.wait_ge(s["x1"], tl + 1)
                act.drain()
                act.activation(junk[:], x1[:, tl % 3], ACT.Square, accum_out=ss[:, 1, tl, 0:1]).then_inc(s["ss2"], 1)
                act.wait_ge(s["var2"], tl + 1)
                act.activation(std[:, 1, tl:tl + 1], var[:, 1, tl:tl + 1], ACT.Sqrt)
                act.drain()
                if tl >= 2:
                    act.wait_ge(s_nd[tl % 2], 16 * (tl // 2))
                    act.wait_ge(s["t"], 2 * (tl - 1))
                act.activation(normed[:, tl % 2], x1[:, tl % 3], ACT.Identity, scale=std[:, 1, tl:tl + 1]).then_inc(s["n"], 1)

            def modulate(tl):
                act.wait_ge(s["t"], 2 * tl + 1)
                g = TILE_GROUP[tl]
                if tl >= 2:
                    act.wait_ge(s["l"], tl - 1)
                for c in range(4):
                    ins = act.activation(h2T[:, tl % 2, c], ps_t[0][:, c * P:(c + 1) * P], ACT.Identity,
                                         scale=t.scale2[:, c, g:g + 1], bias=t.shift2[:, c, g:g + 1])
                ins.then_inc(s["ta"], 1)

            for k in range(NT + 2):
                if k < NT:
                    act.drain()
                    squares(k)
                if 1 <= k < NT + 1:
                    norm(k - 1)
                if k >= 2:
                    modulate(k - 2)
            act.wait_ge(s["sm"], 1)
            act.activation(lg[:], lg[:], ACT.Exp).then_inc(s["exp"], 1)

        @block.vector
        def _(dve):
            def variance(k, tl):
                v = var[:, k, tl:tl + 1]
                dve.wait_ge(s["ss" if k == 0 else "ss2"], tl + 1)
                if k == 0:
                    dve.tensor_tensor(v, ss[:, 0, tl, 0:1], ss[:, 0, tl, 1:2], ALU.add)
                    dve.drain()
                dve.tensor_scalar(v, v if k == 0 else ss[:, 1, tl, 0:1], 1.0 / D, EPS, ALU.mult, ALU.add)
                dve.drain()
                dve.reciprocal(v, v).then_inc(s["var" if k == 0 else "var2"], 1)

            def scaled(tl):
                g = TILE_GROUP[tl]
                dve.wait_ge(s["std"], tl + 1)
                if tl >= 3:
                    dve.wait_ge(s_x1d[tl % 3], 16 * (tl // 3))
                    dve.wait_ge(s["n"], tl - 2)
                for hf in range(2):
                    sl = slice(hf * 512, (hf + 1) * 512)
                    ins = dve.scalar_tensor_tensor(out=x1[:, tl % 3, sl], in0=ps_o[tl % 2][hf][:],
                                                   scalar=std[:, 0, tl:tl + 1], in1=gate[:, g, sl],
                                                   op0=ALU.mult, op1=ALU.mult)
                dve.drain()
                dve.sem_inc(s["scaled"], 1)

            def modulate(tl):
                dve.wait_ge(s["t"], 2 * tl + 2)
                g = TILE_GROUP[tl]
                if tl >= 2:
                    dve.wait_ge(s["l"], tl - 1)
                for c in range(4):
                    ins = dve.tensor_scalar(h2T[:, tl % 2, 4 + c], ps_t[1][:, c * P:(c + 1) * P],
                                            t.scale2[:, 4 + c, g:g + 1], t.shift2[:, 4 + c, g:g + 1], ALU.mult, ALU.add)
                ins.then_inc(s["tv"], 1)

            def logits(tl):
                dve.wait_ge(s["l"], tl + 1)
                dve.tensor_copy(lgT[:, tl * P:(tl + 1) * P], ps_l[tl % 2][0:NE, 0:P]).then_inc(s["lc"], 1)

            dve.wait_ge(t.s_next, 48)
            for k in range(NT + 3):
                if k < NT:
                    variance(0, k)
                    scaled(k)
                if 1 <= k < NT + 1:
                    variance(1, k - 1)
                if 2 <= k < NT + 2:
                    modulate(k - 2)
                if k >= 3:
                    logits(k - 3)
            dve.wait_ge(s["lt"], 1)
            lp = ps_l[0][:, 0:NT * NE].rearrange("p (t e) -> p t e", e=NE)
            dve.tensor_reduce(mx[:], lp, AX_X, ALU.max)
            dve.drain()
            dve.tensor_tensor(lg[:], lp, mx[:].unsqueeze(2).to_broadcast([P, NT, NE]), ALU.subtract).then_inc(s["sm"], 1)
            dve.wait_ge(s["exp"], 1)
            dve.tensor_reduce(mx[:], lg[:], AX_X, ALU.add)
            dve.drain()
            dve.reciprocal(mx[:], mx[:])
            dve.drain()
            dve.tensor_tensor(lg[:], lg[:], mx[:].unsqueeze(2).to_broadcast([P, NT, NE]), ALU.mult).then_inc(s["aff"], 1)
            for g, (o, m) in enumerate(BLKS):
                bank = [ps_o[0][0], ps_o[0][1], ps_o[1][0]][g]
                dve.wait_ge(s["at"], g + 1)
                dve.tensor_copy(affT[:, o:o + m], bank[0:NE, 0:m]).then_inc(s["done"], 1)


def expert_load(eng, t, ring, slot, e, j, sem):
    eng.dma_start(ring[:, slot, 0:8].rearrange("p k f -> p k f"), t.w_gate_v[e][:, j]).then_inc(sem, 16)
    eng.dma_start(ring[:, slot, 8:16], t.w_up_v[e][:, j]).then_inc(sem, 16)
    eng.dma_start(ring[:, slot, 16:24].rearrange("p (c k) f -> p c (k f)", c=2), t.w_down_v[e][:, j]).then_inc(sem, 16)


def phase_choice(nc, t):
    with ExitStack() as ctx:
        sb = lambda n, s, d=F32: ctx.enter_context(nc.sbuf_tensor(n, s, d))
        sem = lambda n: ctx.enter_context(nc.semaphore("c_" + n))
        CS, CP = CAPS[1], CAPS[0]
        HALF = SEQS[1] // 2
        R = 3 * NE
        aff = sb("aff", [R, HALF])
        best = sb("best", [R, CS])
        found = sb("found", [R, CS], U32)
        foundf = sb("foundf", [R, CS])
        flip = sb("flip", [P, P])
        cols = sb("cols_c", [P, 2, R])
        first = sb("first", [P, NE])
        place = sb("place", [P, NE])
        ps = ctx.enter_context(nc.psum_tensor("ps_c", [P, 512], F32))
        ps_b = ctx.enter_context(nc.psum_tensor("ps_cb", [P, 512], F32))
        s_a, s_flip, s_f, s_t, s_cols, s_b = (sem(n) for n in ("a", "flip", "f", "t", "cols", "b"))
        block = ctx.enter_context(nc.Block())

        @block.sync
        def _(sp):
            for h in range(2):
                o = SEQS[0] + h * HALF
                sp.dma_start(aff[h * NE:(h + 1) * NE], t.aff_dram[:, o:o + HALF]).then_inc(s_a, 16)
            sp.dma_start(aff[2 * NE:R, 0:SEQS[0]], t.aff_dram[:, 0:SEQS[0]]).then_inc(s_a, 16)
            sp.dma_start(flip[:], t.c_flip).then_inc(s_flip, 16)
            for j in range(4):
                expert_load(sp, t, t.ring, j, 0, j, t.s_ring[j])

        @block.vector
        def _(dve):
            dve.memset(aff[2 * NE:R, SEQS[0]:HALF], -1.0)
            dve.drain()
            dve.wait_ge(s_a, 48)
            for k in range(0, CS, 8):
                v = best[:, k:k + 8]
                dve.max(out=v, in_=aff[:])
                dve.drain()
                dve.max_index(out=found[:, k:k + 8], in_max=v, in_values=aff[:])
                dve.match_replace(out=aff[:], in_to_replace=v, in_values=aff[:], imm_value=-1.0)
                dve.drain()
            dve.tensor_copy(foundf[:], found[:])
            dve.drain()
            dve.sem_inc(s_f, 1)
            dve.wait_ge(s_t, 1)
            dve.tensor_copy(cols[:], ps[:, 0:2 * R].rearrange("p (k r) -> p k r", k=2)).then_inc(s_cols, 1)
            dve.drain()
            dve.tensor_copy(t.gate_p[:, 0:NE], cols[0:CP, 0, 2 * NE:R])
            dve.tensor_copy(t.idx_p[:, 0:NE], cols[0:CP, 1, 2 * NE:R])
            dve.tensor_copy(t.idx_p[:, NE:NE + 1], cols[0:CP, 1, 2 * NE:2 * NE + 1])
            dve.wait_ge(s_b, 1)
            a, b = cols[:, 0, 0:NE], ps_b[:, 0:NE]
            a_at, b_at = cols[:, 1, 0:NE], ps_b[:, NE:2 * NE]
            dve.tensor_tensor(first[:], a, b, ALU.is_ge)
            dve.tensor_tensor(t.gate_s[:, 0:NE], a, b, ALU.max)
            dve.tensor_tensor(place[:], a_at, b_at, ALU.subtract)
            dve.drain()
            dve.tensor_scalar(place[:], place[:], float(-HALF), None, ALU.add)
            dve.drain()
            dve.tensor_tensor(place[:], place[:], first[:], ALU.mult)
            dve.drain()
            dve.tensor_tensor(place[:], place[:], b_at, ALU.add)
            dve.drain()
            dve.tensor_scalar(t.idx_s[:, 0:NE], place[:], float(SEQS[0] + HALF), None, ALU.add)
            dve.tensor_scalar(t.idx_s[:, NE:NE + 1], place[:, 0:1], float(SEQS[0] + HALF), None, ALU.add)

        @block.tensor
        def _(pe):
            pe.wait_ge(s_f, 1)
            pe.transpose(ps[:, 0:R], best[:], t.ident[0:R, 0:R])
            pe.transpose(ps[:, R:2 * R], foundf[:], t.ident[0:R, 0:R]).then_inc(s_t, 1)
            pe.wait_ge(s_flip, 16)
            pe.wait_ge(s_cols, 1)
            for k in range(2):
                mm = pe.matmul(ps_b[:, k * NE:(k + 1) * NE], flip[:], cols[:, k, NE:2 * NE], start=True, stop=True)
            mm.then_inc(s_b, 1)


def phase_experts(nc, t):
    CS, CP = CAPS[1], CAPS[0]
    NJ = DE // 256
    NQ = 2 * NJ
    with ExitStack() as ctx:
        sb = lambda n, s, d=F32: ctx.enter_context(nc.sbuf_tensor(n, s, d))
        sem = lambda n: ctx.enter_context(nc.semaphore("e_" + n))
        psum = lambda n: ctx.enter_context(nc.psum_tensor(n, [P, 512], F32))
        rows_s = sb("rows_s", [CS, D])
        rows_p = sb("rows_p", [CP, D])
        xT = sb("xT", [P, KC, CAPT])
        silu = sb("silu", [P, 2, CAPT])
        hid = sb("hid", [P, 2, CAPT])
        yT = sb("yT_e", [P, KC, CAPT])
        out_s = sb("out_s", [CS, D])
        out_p = sb("out_p", [CP, D])
        tick = sb("tick", [1, 2])
        gate_s = sb("gate_now_s", [CS, 1])
        gate_p = sb("gate_now_p", [CP, 1])
        next_s, next_p = sb("next_s", [CS, 1], U32), sb("next_p", [CP, 1], U32)
        now_s, now_p = sb("now_s", [CS, 1], U32), sb("now_p", [CP, 1], U32)
        ps_gu = [psum(f"ps_gu{i}") for i in range(2)]
        ps_y = [psum(f"ps_ye{i}") for i in range(3)]
        ps_t = [psum(f"ps_te{i}") for i in range(3)]
        out_banks = ps_t + [ps_gu[1]]
        s_rows = sem("rows")
        s_gu = sem("gu")
        s_silu = sem("silu")
        s_hid = sem("hid")
        s_down = sem("down")
        s_xt = sem("xt")
        s_xact, s_xdve = sem("xact"), sem("xdve")
        s_yact, s_ydve = sem("yact"), sem("ydve")
        s_yt = sem("yt")
        s_oact, s_odve = sem("oact"), sem("odve")
        s_gate = sem("gate")
        s_last = sem("last")
        s_add = sem("add")
        s_stored = sem("stored")

        def chunks(bank):
            return range(3 * bank, min(3 * bank + 3, KC))

        block = ctx.enter_context(nc.Block())

        @block.sync
        def _(sp):
            with sp.Fori(0, NE - 1) as e:
                for j in range(NJ):
                    sp.wait_ge(s_down, e * NQ + 2 * (j + 1))
                    expert_load(sp, t, t.ring, j % 4, e if j < 4 else e + 1, (j + 4) % NJ, t.s_ring[j % 4])
            sp.dma_start(t.gate2[:], t.gates_dram[1].unsqueeze(0).to_broadcast([P, 2, D])).then_inc(s_last, 16)
            sp.dma_start(t.x1_sb[:], t.x1_dram.rearrange("(t p) d -> p t d", p=P)).then_inc(s_last, 16)
            for j in range(4):
                sp.wait_ge(s_down, (NE - 1) * NQ + 2 * (j + 1))
                expert_load(sp, t, t.ring, j, NE - 1, j + 4, t.s_ring[j])
            sp.wait_ge(s_last, 32)

        @block.gpsimd
        def _(pool):
            def take_waits():
                pool.tensor_tensor(tick[:, 1:2], tick[:, 0:1], tick[:, 0:1], ALU.add)
                pool.drain()

            def gather():
                take_waits()
                fetch()

            def fetch():
                pool.indirect_dma_start(out=rows_s[:], out_offset=None, in_=t.xn_dram,
                                        in_offset=bass.IndirectOffsetOnAxis(ap=next_s[:, 0:1], axis=0)).then_inc(s_rows, 16)
                pool.indirect_dma_start(out=rows_p[:], out_offset=None, in_=t.xn_dram,
                                        in_offset=bass.IndirectOffsetOnAxis(ap=next_p[:, 0:1], axis=0)).then_inc(s_rows, 16)

            pool.memset(tick[:], 0.0)
            pool.sem_inc(s_stored, 1)
            pool.tensor_copy(next_s[:], t.idx_s[:, 0:1])
            pool.tensor_copy(next_p[:], t.idx_p[:, 0:1])
            pool.drain()
            fetch()
            with pool.Fori(0, NE) as e:
                pool.wait_ge(s_rows, e * 32 + 32)
                pool.tensor_copy(next_s[:], t.idx_s[:, bass.ds(e + 1, 1)])
                pool.tensor_copy(next_p[:], t.idx_p[:, bass.ds(e + 1, 1)])
                pool.wait_ge(s_xt, e * 3 + 3)
                gather()
                pool.tensor_copy(now_s[:], t.idx_s[:, bass.ds(e, 1)])
                pool.tensor_copy(now_p[:], t.idx_p[:, bass.ds(e, 1)])
                pool.drain()
                pool.wait_ge(s_oact, e * 2 + 3)
                pool.wait_ge(s_odve, e * 2 + 3)
                take_waits()
                pool.indirect_dma_start(out=t.moe_dram, out_offset=bass.IndirectOffsetOnAxis(ap=now_s[:, 0:1], axis=0),
                                        in_=out_s[:], in_offset=None, compute_op=ALU.add).then_inc(s_add, 16)
                pool.indirect_dma_start(out=t.moe_dram, out_offset=bass.IndirectOffsetOnAxis(ap=now_p[:, 0:1], axis=0),
                                        in_=out_p[:], in_offset=None, compute_op=ALU.add).then_inc(s_add, 16)
                pool.wait_ge(s_add, e * 32 + 32)
                take_waits()
                pool.sem_inc(s_stored, 1)

        @block.tensor
        def _(pe):
            def turn_rows(bank):
                for k, c in enumerate(chunks(bank)):
                    o = k * CAPT
                    pe.transpose(ps_t[bank][:, o:o + CS], rows_s[:, c * P:(c + 1) * P], t.ident[:])
                    mm = pe.transpose(ps_t[bank][:, o + CS:o + CAPT], rows_p[:, c * P:(c + 1) * P], t.ident[0:CP, 0:CP])
                mm.then_inc(s_xt, 1)

            def gate_up(q, e):
                j, f = divmod(q, 2)
                w = t.ring[:, j % 4]
                if f == 0:
                    pe.wait_ge(t.s_ring[j % 4], e * 96 + 48 * (j // 4 + 1))
                pe.wait_ge(s_hid, e * NQ + (q + 1))
                if q == 1:
                    pe.wait_ge(s_odve, e * 2 + 1)
                for m in range(2):
                    for c in range(KC):
                        mm = pe.matmul(ps_gu[q % 2][:, m * CAPT:(m + 1) * CAPT], w[:, 8 * m + c, f * P:(f + 1) * P],
                                       xT[:, c], start=(c == 0), stop=(c == KC - 1))
                mm.then_inc(s_gu, 1)

            def down(q, e):
                j, f = divmod(q, 2)
                w = t.ring[:, j % 4, 16 + 4 * f:20 + 4 * f].rearrange("p k f -> p (k f)")
                pe.wait_ge(s_hid, e * NQ + (q + 3))
                for c in range(KC):
                    o = c % 3 * CAPT
                    mm = pe.matmul(ps_y[c // 3][:, o:o + CAPT], w[:, c * P:(c + 1) * P], hid[:, q % 2],
                                   start=(q == 0 and c % 3 == 0), stop=(q == NQ - 1), skip_group_check=True)
                mm.then_inc(s_down, 1)

            pe.wait_ge(s_rows, 32)
            for bank in range(3):
                turn_rows(bank)
            with pe.Fori(0, NE) as e:
                pe.wait_ge(s_xact, e * 2 + 2)
                pe.wait_ge(s_xdve, e + 1)
                for q in range(NQ):
                    gate_up(q, e)
                    if q >= 1:
                        down(q - 1, e)
                pe.wait_ge(s_rows, e * 32 + 64)
                pe.wait_ge(s_oact, e * 2 + 1)
                pe.wait_ge(s_odve, e * 2 + 1)
                turn_rows(0)
                turn_rows(1)
                down(NQ - 1, e)
                turn_rows(2)
                pe.wait_ge(s_yact, e + 1)
                for k in range(4):
                    bank = out_banks[k]
                    if k < 2:
                        pe.wait_ge(s_ydve, e * 2 + (k + 1))
                    if k in (0, 2):
                        pe.wait_ge(s_xact, e * 2 + (3 + k // 2))
                    elif k == 1:
                        pe.wait_ge(s_xdve, e + 2)
                    n, o = (CS, 0) if k < 2 else (CP, CS)
                    for c in range(4):
                        mm = pe.transpose(bank[0:n, c * P:(c + 1) * P], yT[:, 4 * (k % 2) + c, o:o + n], t.ident[:])
                    mm.then_inc(s_yt, 1)

        def rows_to_xT(eng, bank, act):
            for k, c in enumerate(chunks(bank)):
                for g, (o, n) in ((1, (0, CS)), (0, (CS, CP))):
                    dst, src = xT[:, c, o:o + n], ps_t[bank][:, k * CAPT + o:k * CAPT + o + n]
                    a, b = t.scale2[:, c, g:g + 1], t.shift2[:, c, g:g + 1]
                    ins = eng.activation(dst, src, ACT.Identity, scale=a, bias=b) if act else \
                        eng.tensor_scalar(dst, src, a, b, ALU.mult, ALU.add)
            return ins

        @block.scalar
        def _(act):
            act.sem_inc(s_oact, 1)
            act.wait_ge(s_xt, 1)
            rows_to_xT(act, 0, True).then_inc(s_xact, 1)
            act.wait_ge(s_xt, 3)
            rows_to_xT(act, 2, True).then_inc(s_xact, 1)
            with act.Fori(0, NE) as e:
                for q in range(NQ):
                    act.wait_ge(s_gu, e * NQ + (q + 1))
                    act.activation(silu[:, q % 2], ps_gu[q % 2][:, 0:CAPT], ACT.Silu).then_inc(s_silu, 1)
                act.wait_ge(s_xt, e * 3 + 4)
                rows_to_xT(act, 0, True).then_inc(s_xact, 1)
                act.wait_ge(s_down, e * NQ + NQ)
                act.activation(yT[:, 3:6], ps_y[1][:, 0:3 * CAPT].rearrange("p (c n) -> p c n", c=3),
                               ACT.Copy).then_inc(s_yact, 1)
                act.wait_ge(s_xt, e * 3 + 6)
                rows_to_xT(act, 2, True).then_inc(s_xact, 1)
                act.wait_ge(s_gate, e + 1)
                act.wait_ge(s_stored, e + 1)
                act.wait_ge(s_yt, e * 4 + 1)
                act.activation(out_s[:, 0:512], ps_t[0][:], ACT.Identity, scale=gate_s[:, 0:1]).then_inc(s_oact, 1)
                act.wait_ge(s_yt, e * 4 + 3)
                act.activation(out_p[:, 0:512], ps_t[2][0:CP, :], ACT.Identity, scale=gate_p[:, 0:1]).then_inc(s_oact, 1)

        @block.vector
        def _(dve):
            dve.sem_inc(s_hid, 2)
            dve.sem_inc(s_odve, 1)
            dve.wait_ge(s_xt, 2)
            rows_to_xT(dve, 1, False).then_inc(s_xdve, 1)
            with dve.Fori(0, NE) as e:
                for q in range(NQ):
                    dve.wait_ge(s_silu, e * NQ + (q + 1))
                    dve.tensor_tensor(hid[:, q % 2], silu[:, q % 2], ps_gu[q % 2][:, CAPT:2 * CAPT],
                                      ALU.mult).then_inc(s_hid, 1)
                dve.wait_ge(s_oact, e * 2 + 1)
                dve.tensor_copy(gate_s[:], t.gate_s[:, bass.ds(e, 1)])
                dve.tensor_copy(gate_p[:], t.gate_p[:, bass.ds(e, 1)])
                dve.drain()
                dve.sem_inc(s_gate, 1)
                dve.wait_ge(s_xt, e * 3 + 5)
                rows_to_xT(dve, 1, False).then_inc(s_xdve, 1)
                dve.wait_ge(s_down, e * NQ + NQ)
                dve.tensor_copy(yT[:, 0:3], ps_y[0][:, 0:3 * CAPT].rearrange("p (c n) -> p c n", c=3)).then_inc(s_ydve, 1)
                dve.tensor_copy(yT[:, 6:8], ps_y[2][:, 0:2 * CAPT].rearrange("p (c n) -> p c n", c=2)).then_inc(s_ydve, 1)
                dve.wait_ge(s_stored, e + 1)
                dve.wait_ge(s_yt, e * 4 + 2)
                dve.tensor_scalar(out_s[:, 512:D], ps_t[1][:], gate_s[:, 0:1], None, ALU.mult).then_inc(s_odve, 1)
                dve.wait_ge(s_yt, e * 4 + 4)
                dve.tensor_scalar(out_p[:, 512:D], ps_gu[1][0:CP, :], gate_p[:, 0:1], None, ALU.mult).then_inc(s_odve, 1)


def phase_output(nc, t):
    with ExitStack() as ctx:
        sb = lambda n, s, d=F32: ctx.enter_context(nc.sbuf_tensor(n, s, d))
        sem = lambda n: ctx.enter_context(nc.semaphore("o_" + n))
        moe = sb("moe", [P, NT, D])
        x1, gate = t.x1_sb, t.gate2
        junk = sb("junk_o", [P, D])
        ss = sb("ss_o", [P, NT])
        s_ss, s_var, s_std, s_moe, s_y, s_st = (sem(n) for n in ("ss", "var", "std", "moe", "y", "st"))
        s_m = [sem(f"m{i}") for i in range(NT // 2)]
        outs = [t.y_prompt[0], t.y_sample[0]]
        block = ctx.enter_context(nc.Block())

        @block.sync
        def _(sp):
            for k in range(NT // 2):
                sl = slice(2 * k, 2 * k + 2)
                sp.dma_start(moe[:, sl], t.moe_dram.rearrange("(t p) d -> p t d", p=P)[:, sl]).then_inc(s_m[k], 16)
            for tl in range(NT):
                g = TILE_GROUP[tl]
                o = (tl - FIRST_TILE[g]) * P
                sp.wait_ge(s_y, tl + 1)
                sp.dma_start(outs[g][o:o + P], x1[:, tl]).then_inc(s_st, 16)
            sp.wait_ge(s_st, 16 * NT)

        @block.scalar
        def _(act):
            def root(tl):
                act.wait_ge(s_var, tl + 1)
                act.activation(ss[:, tl:tl + 1], ss[:, tl:tl + 1], ACT.Sqrt).then_inc(s_std, 1)

            for tl in range(NT):
                act.wait_ge(s_m[tl // 2], 16)
                act.drain()
                act.activation(junk[:], moe[:, tl], ACT.Square, accum_out=ss[:, tl:tl + 1]).then_inc(s_ss, 1)
                if tl >= 1:
                    root(tl - 1)
            root(NT - 1)

        @block.vector
        def _(dve):
            def variance(tl):
                v = ss[:, tl:tl + 1]
                dve.wait_ge(s_ss, tl + 1)
                dve.tensor_scalar(v, v, 1.0 / D, EPS, ALU.mult, ALU.add)
                dve.drain()
                dve.reciprocal(v, v).then_inc(s_var, 1)

            variance(0)
            for tl in range(NT):
                if tl + 1 < NT:
                    variance(tl + 1)
                dve.wait_ge(s_std, tl + 1)
                dve.scalar_tensor_tensor(out=moe[:, tl], in0=moe[:, tl], scalar=ss[:, tl:tl + 1],
                                         in1=gate[:, TILE_GROUP[tl]], op0=ALU.mult, op1=ALU.mult).then_inc(s_moe, 1)

        @block.gpsimd
        def _(pool):
            for tl in range(NT):
                pool.wait_ge(s_moe, tl + 1)
                pool.tensor_tensor(x1[:, tl], x1[:, tl], moe[:, tl], ALU.add).then_inc(s_y, 1)


class Tensors:
    pass


def build_program(nc, ins, outs):
    t = Tensors()
    t.x_prompt, t.x_sample, t.c_prompt, t.c_sample = (ins["x_prompt"], ins["x_sample"], ins["c_prompt"], ins["c_sample"])
    t.w_ada, t.b_ada, t.g_pre1, t.g_post1 = (ins["w_ada"], ins["b_ada"], ins["g_pre1"], ins["g_post1"])
    t.w_in, t.gn_ret, t.gn_hg, t.lb_logits = (ins["w_in"], ins["gn_ret"], ins["gn_hg"], ins["lb_logits"])
    t.w_br_ret, t.w_br_hg, t.w_out, t.g_pre2 = (ins["w_br_ret"], ins["w_br_hg"], ins["w_out"], ins["g_pre2"])
    t.g_post2, t.w_router, t.w_gate, t.w_up = (ins["g_post2"], ins["w_router"], ins["w_gate"], ins["w_up"])
    t.w_down, t.c_ident, t.c_rot, t.c_ret = (ins["w_down"], ins["c_ident"], ins["c_rot"], ins["c_ret"])
    t.c_masks, t.c_leaves, t.c_flip = ins["c_masks"], ins["c_leaves"], ins["c_flip"]
    t.y_prompt, t.y_sample = outs["y_prompt"], outs["y_sample"]
    scratch = lambda n, s: nc.dram_tensor(n, s, F32).ap()
    t.gates_dram = scratch("gates_dram", (2, 2, D))
    t.yT_dram = scratch("yT_dram", (2, HEADS, P, NTOK))
    t.sig_dram = scratch("sig_dram", (KC, P, 2, NTOK))
    t.x1_dram = scratch("x1_dram", (NTOK, D))
    t.xn_dram = scratch("xn_dram", (NTOK, D))
    t.moe_dram = scratch("moe_dram", (NTOK, D))
    t.aff_dram = scratch("aff_dram", (NE, NTOK))
    t.w_gate_v, t.w_up_v = (w[0].rearrange("e (k p) (j f) -> e p j k f", p=P, f=256) for w in (t.w_gate, t.w_up))
    t.w_down_v = t.w_down[0].rearrange("e (j c p) d -> e p j c d", p=P, c=2)
    with ExitStack() as ctx:
        sb = lambda n, s, d=F32: ctx.enter_context(nc.sbuf_tensor(n, s, d))
        t.ident = sb("ident", [P, P])
        t.scale1, t.shift1 = sb("scale1", [P, KC, 2]), sb("shift1", [P, KC, 2])
        t.scale2, t.shift2 = sb("scale2", [P, KC, 2]), sb("shift2", [P, KC, 2])
        t.head_cols = sb("head_cols", [P, HEADS, 4])
        with ExitStack() as mix:
            t.hT = mix.enter_context(nc.sbuf_tensor("hT", [P, KC, NTOK], F32))
            with ExitStack() as heads:
                hsb = lambda n, s, d=F32: heads.enter_context(nc.sbuf_tensor(n, s, d))
                t.w_head = hsb("w_head", [P, KC, NCOLG, P])
                t.rot = hsb("rot", [P, SEQS[1] // P, 2, 64])
                t.masks = hsb("masks", [P, 2 * len(LEVELS), P], U8)
                t.leaves = hsb("leaves", [P, 2, P])
                t.ones = hsb("ones", [P, P])
                phase_modulation(nc, t)
                phase_heads(nc, t)
            t.yT = t.hT[:].rearrange("p (m h) n -> p m h n", m=2)
            t.w_br = mix.enter_context(nc.sbuf_tensor("w_br", [P, 2, 2, HEADS, P], F32))
            t.w_br_v = [w[0].rearrange("(h p) (o x) -> o p h x", p=P, o=KC) for w in (t.w_br_ret, t.w_br_hg)]
            t.s_branch = mix.enter_context(nc.semaphore("branch"))
            t.s_branch1 = mix.enter_context(nc.semaphore("branch1"))
            phase_branch_gates(nc, t)
            t.mergedT = mix.enter_context(nc.sbuf_tensor("mergedT", [P, KC, NTOK], F32))
            t.w_out_sb = mix.enter_context(nc.sbuf_tensor("w_out_sb", [P, KC, D], F32))
            t.w_r = mix.enter_context(nc.sbuf_tensor("w_r", [P, KC, NE], F32))
            t.gate1 = mix.enter_context(nc.sbuf_tensor("gate1", [P, 2, D], F32))
            t.s_next = mix.enter_context(nc.semaphore("next"))
            phase_merge(nc, t)
            phase_residual(nc, t)
        t.ring = sb("ring", [P, 4, 24, 256])
        t.s_ring = [ctx.enter_context(nc.semaphore(f"ring{i}")) for i in range(4)]
        t.gate_s, t.gate_p = sb("gate_s", [CAPS[1], NE]), sb("gate_p", [CAPS[0], NE])
        t.idx_s, t.idx_p = sb("idx_s", [CAPS[1], NE + 1], U32), sb("idx_p", [CAPS[0], NE + 1], U32)
        phase_choice(nc, t)
        t.x1_sb, t.gate2 = sb("x1_sb", [P, NT, D]), sb("gate2", [P, 2, D])
        phase_experts(nc, t)
        phase_output(nc, t)


_INS = ["x_prompt", "x_sample", "c_prompt", "c_sample", "w_ada", "b_ada", "g_pre1", "g_post1", "w_in", "gn_ret",
        "gn_hg", "lb_logits", "w_br_ret", "w_br_hg", "w_out", "g_pre2", "g_post2", "w_router", "w_gate", "w_up", "w_down"]


def kernel(**inputs):
    import concourse.bacc as _bacc
    from concourse.bass_utils import run_bass_kernel_spmd as _run

    nc = _bacc.Bacc("TRN2", target_bir_lowering=False, num_devices=1)
    arrays, ins, outs = {}, {}, {}
    for prefix, group in (("in_", {n: inputs[n] for n in _INS}), ("const_", shape_constants())):
        for name, a in group.items():
            a = np.ascontiguousarray(a)
            arrays[prefix + name] = a
            key = name if prefix == "in_" else "c_" + name
            ins[key] = nc.dram_tensor(prefix + name, a.shape, mybir.dt.from_np(a.dtype), kind="ExternalInput").ap()
    for name, s in (("y_prompt", SEQS[0]), ("y_sample", SEQS[1])):
        outs[name] = nc.dram_tensor("out_" + name, (1, s, D), F32, kind="ExternalOutput").ap()
    build_program(nc, ins, outs)
    r = _run(nc, [arrays], core_ids=[0])
    return tuple(r.results[0]["out_" + name] for name in ("y_prompt", "y_sample"))
```
